# Optimizing a Trainium2 kernel written in Bass

```python
import math
import jax, jax.numpy as jnp
from jax import lax
import numpy as np

D_MODEL = 1024
BATCH = 1
SEQ = 128
DEPTH = 2
DEC_BATCH = 1
DEC_SEQ = 512
PAST_LEN = 128

GRID_W = 64
H_A = 4
D_A = 64
H_B = 4
D_B = 128
CONV_K = 5
CHUNK = 64
H_C = 4
D_C = 128
WIN_R = 8
WIN_C = 16
N_EXPERTS = 16
D_EXPERT = 1024
EC_FACTOR = 2
Q_BLOCK = 128
ROPE_BASE = 10000.0
EPS = 1e-6
NEG = -1e30

W_A = H_A * 2 * D_A
W_B = H_B * D_B
W_C = H_C * D_C
SPLIT_SIZES = (W_A, W_A, W_A,
               W_B, W_B, W_B, W_B,
               2 * H_B, 2 * H_B,
               W_C, W_C, W_C,
               D_MODEL, D_MODEL, D_MODEL)
D_IN = 3 * W_A + 4 * W_B + 4 * H_B + 3 * W_C + 3 * D_MODEL

kernel_name = 'hybrid_diffusion_prefix_trunk_step'

def rmsnorm(x, g):
    xf = x.astype(jnp.float32)
    y = xf * lax.rsqrt(jnp.mean(xf * xf, axis=-1, keepdims=True) + EPS)
    return (y * g.astype(jnp.float32)).astype(x.dtype)

def l2norm(x):
    xf = x.astype(jnp.float32)
    return xf * lax.rsqrt(jnp.sum(xf * xf, axis=-1, keepdims=True) + EPS)

def split_cols(u):
    out, start = [], 0
    for s in SPLIT_SIZES:
        out.append(u[..., start:start + s])
        start += s
    return out

def lambda_init(layer):
    return 0.8 - 0.6 * math.exp(-0.3 * layer)

def axial_rope(x):
    T = x.shape[1]
    quarter = x.shape[-1] // 4
    inv = 1.0 / (ROPE_BASE ** (jnp.arange(quarter, dtype=jnp.float32) / quarter))
    t = jnp.arange(T)
    pos = jnp.stack([t // GRID_W, t % GRID_W], axis=-1).astype(jnp.float32)
    ang = pos[:, :, None] * inv
    bshape = (1, T) + (1,) * (x.ndim - 3) + (2, quarter)
    cos = jnp.cos(ang).reshape(bshape).astype(x.dtype)
    sin = jnp.sin(ang).reshape(bshape).astype(x.dtype)
    xr = x.reshape(x.shape[:-1] + (2, 2, quarter))
    x1, x2 = xr[..., 0, :], xr[..., 1, :]
    return jnp.stack([x1 * cos - x2 * sin, x2 * cos + x1 * sin], axis=-2).reshape(x.shape)

def diff_attention(q, k, v, lam, g_sub, lam_init):
    B, Tq = q.shape[:2]
    scale = D_A ** -0.5
    qb = q.reshape((B, Tq // Q_BLOCK, Q_BLOCK) + q.shape[2:]).swapaxes(0, 1)

    def block(qi):
        s = jnp.einsum('bqhcd,bkhcd->bhcqk', qi, k).astype(jnp.float32) * scale
        p = jax.nn.softmax(s, axis=-1)
        a = p[:, :, 0] - lam * p[:, :, 1]
        return jnp.einsum('bhqk,bkhe->bqhe', a.astype(v.dtype), v)

    o = lax.map(block, qb).swapaxes(0, 1).reshape(B, Tq, H_A, 2 * D_A)
    o = rmsnorm(o, g_sub) * (1.0 - lam_init)
    return o.reshape(B, Tq, W_A)

def dense_attention(q, k, v):
    B, T, H, D = q.shape
    scale = D ** -0.5
    qb = q.reshape(B, T // Q_BLOCK, Q_BLOCK, H, D).swapaxes(0, 1)

    def block(qi):
        s = jnp.einsum('bqhd,bkhd->bhqk', qi, k).astype(jnp.float32) * scale
        p = jax.nn.softmax(s, axis=-1).astype(v.dtype)
        return jnp.einsum('bhqk,bkhd->bqhd', p, v)

    return lax.map(block, qb).swapaxes(0, 1).reshape(B, T, H * D)

def neighborhood_attention(q, k, v, k_ctx, v_ctx, rpb):
    B, T, H, D = q.shape
    rows = T // GRID_W
    wr = min(WIN_R, rows)
    scale = D ** -0.5
    qg = q.reshape(B, rows, GRID_W, H, D)
    kg = k.reshape(B, rows, GRID_W, H, D)
    vg = v.reshape(B, rows, GRID_W, H, D)
    col = jnp.arange(GRID_W)
    cs = jnp.clip(col - WIN_C // 2, 0, GRID_W - WIN_C)
    col_mask = (col[None, :] >= cs[:, None]) & (col[None, :] < cs[:, None] + WIN_C)
    dc_idx = jnp.clip(col[None, :] - col[:, None] + WIN_C - 1, 0, 2 * WIN_C - 2)

    def row_block(r):
        rs = jnp.clip(r - wr // 2, 0, rows - wr)
        qr = lax.dynamic_index_in_dim(qg, r, axis=1, keepdims=False)
        kb = lax.dynamic_slice_in_dim(kg, rs, wr, axis=1)
        vb = lax.dynamic_slice_in_dim(vg, rs, wr, axis=1)
        s_loc = jnp.einsum('bqhd,biwhd->bhqiw', qr, kb).astype(jnp.float32) * scale
        dr_idx = rs + jnp.arange(wr) - r + (WIN_R - 1)
        bias = rpb.astype(jnp.float32)[:, dr_idx[:, None, None], dc_idx[None, :, :]]
        s_loc = jnp.where(col_mask[None, None, :, None, :], s_loc + bias.transpose(0, 2, 1, 3)[None], NEG)
        s_ctx = jnp.einsum('bqhd,bkhd->bhqk', qr, k_ctx).astype(jnp.float32) * scale
        n_loc = wr * GRID_W
        s = jnp.concatenate([s_loc.reshape(B, H, GRID_W, n_loc), s_ctx], axis=-1)
        p = jax.nn.softmax(s, axis=-1).astype(v.dtype)
        p_loc = p[..., :n_loc].reshape(B, H, GRID_W, wr, GRID_W)
        return (jnp.einsum('bhqiw,biwhd->bqhd', p_loc, vb)
                + jnp.einsum('bhqk,bkhd->bqhd', p[..., n_loc:], v_ctx))

    out = lax.map(row_block, jnp.arange(rows))
    return out.transpose(1, 0, 2, 3, 4).reshape(B, T, H * D)

def short_conv(x, w):
    pad = CONV_K // 2
    return lax.conv_general_dilated(x, w[:, None, :].astype(x.dtype), window_strides=(1,),
                                    padding=[(pad, pad)], dimension_numbers=('NWC', 'WIO', 'NWC'),
                                    feature_group_count=x.shape[-1])

def deltanet_inputs(q, k, v, a, b, conv_w, a_log, dt_bias):
    B, T, _ = q.shape
    qkv = jax.nn.silu(short_conv(jnp.concatenate([q, k, v], axis=-1), conv_w))
    q, k, v = jnp.split(qkv, 3, axis=-1)
    q = l2norm(q.reshape(B, T, H_B, D_B))
    k = l2norm(k.reshape(B, T, H_B, D_B))
    v = v.reshape(B, T, H_B, D_B).astype(jnp.float32)
    a = a.reshape(B, T, 2, H_B).astype(jnp.float32)
    g = -jnp.exp(a_log.astype(jnp.float32)) * jax.nn.softplus(a + dt_bias.astype(jnp.float32))
    beta = jax.nn.sigmoid(b.reshape(B, T, 2, H_B).astype(jnp.float32))
    return q, k, v, g, beta

def gated_delta_chunked(q, k, v, g, beta, s0):
    B, T, H, DK = q.shape
    n = T // CHUNK
    q = q * (DK ** -0.5)
    to_c = lambda t: t.reshape(B, n, CHUNK, H, t.shape[-1]).transpose(1, 0, 3, 2, 4)
    q, k, v = to_c(q), to_c(k), to_c(v)
    G = jnp.cumsum(g.reshape(B, n, CHUNK, H).transpose(1, 0, 3, 2), axis=-1)
    beta = beta.reshape(B, n, CHUNK, H).transpose(1, 0, 3, 2)
    tri = jnp.tril(jnp.ones((CHUNK, CHUNK), dtype=bool))
    strict = jnp.tril(jnp.ones((CHUNK, CHUNK), dtype=bool), k=-1)
    diff = G[..., :, None] - G[..., None, :]
    decay = jnp.where(tri, jnp.exp(jnp.where(tri, diff, 0.0)), 0.0)
    kb = k * beta[..., None]
    vb = v * beta[..., None]
    L = jnp.where(strict, jnp.einsum('...id,...jd->...ij', kb, k) * decay, 0.0)
    eye = jnp.eye(CHUNK, dtype=jnp.float32)
    Tm = lax.linalg.triangular_solve(eye + L, jnp.broadcast_to(eye, L.shape), left_side=True,
                                     lower=True, unit_diagonal=True)
    u = jnp.einsum('...ij,...jd->...id', Tm, vb)
    w = jnp.einsum('...ij,...jd->...id', Tm, kb * jnp.exp(G)[..., None])
    a_in = jnp.where(tri, jnp.einsum('...id,...jd->...ij', q, k) * decay, 0.0)

    def step(S, xs):
        qi, ki, ui, wi, Gi, Ai = xs
        v_new = ui - jnp.einsum('bhck,bhkv->bhcv', wi, S)
        o = (jnp.einsum('bhck,bhkv->bhcv', qi * jnp.exp(Gi)[..., None], S)
             + jnp.einsum('bhij,bhjv->bhiv', Ai, v_new))
        g_last = Gi[..., -1]
        S = (S * jnp.exp(g_last)[..., None, None]
             + jnp.einsum('bhck,bhcv->bhkv', ki * jnp.exp(g_last[..., None] - Gi)[..., None], v_new))
        return S, o

    s_fin, o = lax.scan(step, s0.astype(jnp.float32), (q, k, u, w, G, a_in))
    return o.transpose(1, 0, 3, 2, 4).reshape(B, T, H, v.shape[-1]), s_fin

def bidir_gated_delta(q, k, v, g, beta, s0_f, s0_b):
    o_f, s_f = gated_delta_chunked(q, k, v, g[:, :, 0], beta[:, :, 0], s0_f)
    rev = lambda t: jnp.flip(t, axis=1)
    o_b, s_b = gated_delta_chunked(rev(q), rev(k), rev(v), rev(g[:, :, 1]), rev(beta[:, :, 1]), s0_b)
    return o_f + rev(o_b), s_f, s_b

def gated_head_norm(o, z, g):
    B, T = z.shape[:2]
    on = rmsnorm(o, g)
    return (on * jax.nn.silu(z.reshape(B, T, H_B, D_B).astype(jnp.float32))).reshape(B, T, W_B).astype(z.dtype)

def expert_choice_ffn(h, w_router, w_gate, w_up, w_down):
    B, T, D = h.shape
    n = B * T
    xt = h.reshape(n, D)
    cap = EC_FACTOR * n // N_EXPERTS
    aff = jax.nn.softmax((xt @ w_router).astype(jnp.float32), axis=-1)
    gate, idx = lax.top_k(aff.T, cap)
    xe = jnp.take(xt, idx, axis=0)
    hid = jax.nn.silu(jnp.einsum('ecd,edf->ecf', xe, w_gate)) * jnp.einsum('ecd,edf->ecf', xe, w_up)
    ye = jnp.einsum('ecf,efd->ecd', hid, w_down) * gate[..., None].astype(h.dtype)
    y = jnp.zeros_like(xt).at[idx.reshape(-1)].add(ye.reshape(-1, D))
    return y.reshape(B, T, D)

def trunk_layer(x, cond, lw, lam_init, ctx=None):
    B, T, _ = x.shape
    mod = (jax.nn.silu(cond) @ lw['w_ada'] + lw['b_ada'])[:, None, :]
    sh1, sc1, gt1, sh2, sc2, gt2 = jnp.split(mod, 6, axis=-1)
    h = rmsnorm(x, lw['g_norm1']) * (1.0 + sc1) + sh1
    (qa, ka, va, qb, kb, vb, zb, ab, bb, qc, kc, vc, ga, gb, gc) = split_cols(h @ lw['w_in'])
    qa = qa.reshape(B, T, H_A, 2, D_A)
    ka = ka.reshape(B, T, H_A, 2, D_A)
    va = va.reshape(B, T, H_A, 2 * D_A)
    qc = qc.reshape(B, T, H_C, D_C)
    kc = kc.reshape(B, T, H_C, D_C)
    vc = vc.reshape(B, T, H_C, D_C)
    lq = lw['lam_qk'].astype(jnp.float32)
    lam = jnp.exp(jnp.sum(lq[0] * lq[1])) - jnp.exp(jnp.sum(lq[2] * lq[3])) + lam_init
    qd, kd, vd, gd, betad = deltanet_inputs(qb, kb, vb, ab, bb, lw['conv_w'], lw['a_log'], lw['dt_bias'])
    if ctx is None:
        oa = diff_attention(qa, ka, va, lam, lw['g_subln'], lam_init)
        s0 = jnp.zeros((B, H_B, D_B, D_B), jnp.float32)
        od, s_f, s_b = bidir_gated_delta(qd, kd, vd, gd, betad, s0, s0)
        oc = dense_attention(qc, kc, vc)
        new_ctx = (ka.reshape(B, T, H_A, 2 * D_A), va, kc, vc,
                   jnp.stack([s_f, s_b], axis=1).astype(x.dtype))
    else:
        ck_a, cv_a, ck_c, cv_c, c_state = ctx
        Lc = ck_a.shape[1]
        k_all = jnp.concatenate([axial_rope(ka), ck_a.reshape(B, Lc, H_A, 2, D_A).astype(ka.dtype)], axis=1)
        v_all = jnp.concatenate([va, cv_a.astype(va.dtype)], axis=1)
        oa = diff_attention(axial_rope(qa), k_all, v_all, lam, lw['g_subln'], lam_init)
        od, _, _ = bidir_gated_delta(qd, kd, vd, gd, betad, c_state[:, 0], c_state[:, 1])
        oc = neighborhood_attention(qc, kc, vc, ck_c.astype(kc.dtype), cv_c.astype(vc.dtype), lw['rpb'])
        new_ctx = None
    ob = gated_head_norm(od, zb, lw['g_onorm'])
    merged = (jax.nn.sigmoid(ga) * (oa @ lw['w_br_a'])
              + jax.nn.sigmoid(gb) * (ob @ lw['w_br_b'])
              + jax.nn.sigmoid(gc) * (oc @ lw['w_br_c']))
    x = x + gt1 * (merged @ lw['w_out'])
    h2 = rmsnorm(x, lw['g_norm2']) * (1.0 + sc2) + sh2
    x = x + gt2 * expert_choice_ffn(h2, lw['w_router'], lw['w_e_gate'], lw['w_e_up'], lw['w_e_down'])
    return x, new_ctx

def setup_inputs(seed: int = 0) -> dict:
    key = jax.random.key(seed)
    keys = iter(jax.random.split(key, 40))

    def nrm(shape, scale):
        return jax.random.normal(next(keys), shape, jnp.float32) * scale

    D = D_MODEL
    dt = jnp.exp(jax.random.uniform(next(keys), (DEPTH, 2, H_B), jnp.float32, math.log(1e-3), math.log(1e-1)))
    return {
        'x_prompt': nrm((BATCH, SEQ, D), 1.0),
        'x_sample': nrm((DEC_BATCH, DEC_SEQ, D), 1.0),
        'c': nrm((DEC_BATCH, D), 1.0),
        'cache_diff_k': nrm((DEC_BATCH, DEPTH, PAST_LEN, H_A, 2 * D_A), 1.0),
        'cache_diff_v': nrm((DEC_BATCH, DEPTH, PAST_LEN, H_A, 2 * D_A), 1.0),
        'cache_na_k': nrm((DEC_BATCH, DEPTH, PAST_LEN, H_C, D_C), 1.0),
        'cache_na_v': nrm((DEC_BATCH, DEPTH, PAST_LEN, H_C, D_C), 1.0),
        'state_delta': nrm((DEC_BATCH, DEPTH, 2, H_B, D_B, D_B), 0.1),
        'c_ctx': nrm((D,), 1.0),
        'w_ada': nrm((DEPTH, D, 6 * D), 0.5 * D ** -0.5),
        'b_ada': nrm((DEPTH, 6 * D), 0.02),
        'g_norm1': 1.0 + nrm((DEPTH, D), 0.02),
        'g_norm2': 1.0 + nrm((DEPTH, D), 0.02),
        'w_in': nrm((DEPTH, D, D_IN), D ** -0.5),
        'conv_w': nrm((DEPTH, CONV_K, 3 * W_B), CONV_K ** -0.5),
        'a_log': jnp.log(jax.random.uniform(next(keys), (DEPTH, 2, H_B), jnp.float32, 1.0, 16.0)),
        'dt_bias': jnp.log(jnp.expm1(dt)),
        'g_onorm': 1.0 + nrm((DEPTH, D_B), 0.02),
        'lam_qk': nrm((DEPTH, 4, D_A), 0.1),
        'g_subln': 1.0 + nrm((DEPTH, 2 * D_A), 0.02),
        'rpb': nrm((DEPTH, H_C, 2 * WIN_R - 1, 2 * WIN_C - 1), 0.1),
        'w_br_a': nrm((DEPTH, W_A, D), W_A ** -0.5),
        'w_br_b': nrm((DEPTH, W_B, D), W_B ** -0.5),
        'w_br_c': nrm((DEPTH, W_C, D), W_C ** -0.5),
        'w_out': nrm((DEPTH, D, D), D ** -0.5),
        'w_router': nrm((DEPTH, D, N_EXPERTS), D ** -0.5),
        'w_e_gate': nrm((DEPTH, N_EXPERTS, D, D_EXPERT), D ** -0.5),
        'w_e_up': nrm((DEPTH, N_EXPERTS, D, D_EXPERT), D ** -0.5),
        'w_e_down': nrm((DEPTH, N_EXPERTS, D_EXPERT, D), D_EXPERT ** -0.5),
        'g_final': 1.0 + nrm((D,), 0.02),
    }

def reference(x_prompt, x_sample, c, cache_diff_k, cache_diff_v, cache_na_k, cache_na_v, state_delta,
              c_ctx, w_ada, b_ada, g_norm1, g_norm2, w_in, conv_w, a_log, dt_bias, g_onorm, lam_qk,
              g_subln, rpb, w_br_a, w_br_b, w_br_c, w_out, w_router, w_e_gate, w_e_up, w_e_down, g_final):
    layers = []
    for l in range(DEPTH):
        layers.append({
            'w_ada': w_ada[l], 'b_ada': b_ada[l], 'g_norm1': g_norm1[l], 'g_norm2': g_norm2[l],
            'w_in': w_in[l], 'conv_w': conv_w[l], 'a_log': a_log[l], 'dt_bias': dt_bias[l],
            'g_onorm': g_onorm[l], 'lam_qk': lam_qk[l], 'g_subln': g_subln[l], 'rpb': rpb[l],
            'w_br_a': w_br_a[l], 'w_br_b': w_br_b[l], 'w_br_c': w_br_c[l], 'w_out': w_out[l],
            'w_router': w_router[l], 'w_e_gate': w_e_gate[l], 'w_e_up': w_e_up[l], 'w_e_down': w_e_down[l],
        })

    cond_ctx = jnp.broadcast_to(c_ctx, (x_prompt.shape[0], D_MODEL))
    xp = x_prompt
    dk_l, dv_l, nk_l, nv_l, st_l = [], [], [], [], []
    for l in range(DEPTH):
        xp, (dk, dv, nk, nv, st) = trunk_layer(xp, cond_ctx, layers[l], lambda_init(l))
        dk_l.append(dk)
        dv_l.append(dv)
        nk_l.append(nk)
        nv_l.append(nv)
        st_l.append(st)
    y_prompt = rmsnorm(xp, g_final)

    xs = x_sample
    for l in range(DEPTH):
        ctx = (cache_diff_k[:, l], cache_diff_v[:, l], cache_na_k[:, l], cache_na_v[:, l], state_delta[:, l])
        xs, _ = trunk_layer(xs, c, layers[l], lambda_init(l), ctx)
    y_sample = rmsnorm(xs, g_final)

    new_diff_k = jnp.stack(dk_l, axis=1)
    new_diff_v = jnp.stack(dv_l, axis=1)
    new_na_k = jnp.stack(nk_l, axis=1)
    new_na_v = jnp.stack(nv_l, axis=1)
    new_state_delta = jnp.stack(st_l, axis=1)
    return (y_prompt, y_sample, new_diff_k, new_diff_v, new_na_k, new_na_v, new_state_delta)


_drawn_inputs = setup_inputs


def setup_inputs(seed=0):
    import zlib

    import numpy as np

    out = dict(_drawn_inputs(seed))
    spreads = {}
    factors = {'cache_na_k': 3.719,
     'cache_na_v': 3.182,
     'state_delta': 3.342,
     'g_norm2': 6.615,
     'g_onorm': 8.0,
     'g_subln': 8.0,
     'rpb': 64.0,
     'g_final': 8.555}
    for name, (base, spread) in spreads.items():
        noise = np.random.default_rng([zlib.crc32(name.encode()), seed]).standard_normal(out[name].shape)
        drawn = base * np.exp(spread * noise) if base else spread * noise
        out[name] = __import__('jax').numpy.asarray(drawn.astype(out[name].dtype))
    for name, factor in factors.items():
        out[name] = (out[name] * factor).astype(out[name].dtype)
    return out
```

```python
import math
from contextlib import ExitStack

import numpy as np
import concourse.bass as bass
from concourse import mybir

F32 = mybir.dt.float32
ALU = mybir.AluOpType
ACT = mybir.ActivationFunctionType
AX = mybir.AxisListType.X

P = 128
D = 1024
KD = D // P
DEPTH = 2
TS, TP = 512, 128
T = TS + TP
NT = T // P
NTS = TS // P
H = 4
BR = H * P
NE, DE = 16, 1024
SLS = 2 * TS // NE
SLP = 2 * TP // NE
SL = SLS + SLP
NPAIR = NE // 2
GRID_W = 64
GROWS = TS // GRID_W
WIN_R, WIN_C = 8, 16
CONV = 5
EPS = 1e-6
NEG = -1e30
RING = 3
PADW = T + 8
SEG = dict(qa=0, ka=512, va=1024, qb=1536, kb=2048, vb=2560, zb=3072, ab=3584,
           qc=3600, kc=4112, vc=4624, ga=5136, gb=6160, gc=7184)

V_BADA, V_G1, V_G2, V_CONV, V_GO, V_GS = 0, 48, 56, 64, 124, 125
V_ROWS = 126

UNITS_OF = dict(ada=1, fm=5, tm=5, br=5)
PLAN = [("ada", a) for a in range(4)]
for _i, _s in enumerate(["qb", "kb", "vb", "zb"]):
    PLAN += [(_s, 0), ("ada", 4 + _i)]
for _i, _s in enumerate(["qa", "ka", "va"]):
    PLAN += [(_s, 0), ("ada", 8 + _i)]
PLAN += [("qc", 0), ("ada", 11), ("kc", 0), ("vc", 0)]
for _s in "abc":
    PLAN += [("g" + _s, 0), ("br" + _s, 0), ("g" + _s, 1), ("br" + _s, 1)]
PLAN += [("wo", 0), ("wo", 1)]


def kind_of(name):
    return "ada" if name == "ada" else "tm" if name in ("va", "vc") else "br" if name.startswith("br") else "fm"


CHUNK_AT, UNIT_AT = {}, {}
_u = 0
for _c, (_n, _i) in enumerate(PLAN):
    CHUNK_AT[_n, _i], UNIT_AT[_n, _i] = _c, _u
    _u += UNITS_OF[kind_of(_n)]
PRE_CHUNKS, PRE_UNITS = len(PLAN), _u
PAIR_CHUNKS, PAIR_UNITS = 12, 14
UNIT_AT["pair", 0] = PRE_UNITS
UNIT_AT["yp", 0] = PRE_UNITS + NPAIR * PAIR_UNITS
UNIT_AT["scatter", 0] = UNIT_AT["yp", 0] + 4
LAYER_UNITS = UNIT_AT["scatter", 0] + KD + 2
LAYER_CHUNKS = PRE_CHUNKS + NPAIR * PAIR_CHUNKS
FIRST_UNITS = KD + 2
assert PRE_CHUNKS % RING == 0 and PAIR_CHUNKS % RING == 0


def unit_no(l, name, i=0, j=0):
    return FIRST_UNITS + l * LAYER_UNITS + UNIT_AT[name, i] + j


def chunk_no(l, name, i=0):
    return l * LAYER_CHUNKS + CHUNK_AT[name, i]


def units_through(c):
    l, q = c // LAYER_CHUNKS, c % LAYER_CHUNKS
    if q < PRE_CHUNKS:
        name, i = PLAN[q]
        return unit_no(l, name, i) + UNITS_OF[kind_of(name)]
    q -= PRE_CHUNKS
    return unit_no(l, "pair") + q // PAIR_CHUNKS * PAIR_UNITS + q % PAIR_CHUNKS + 1


CST = {}
_at = 0
for _n, _w in [("ident", P), ("tri", 2 * P), ("strict", 2 * P), ("blk16", P), ("m32", P), ("m64", P), ("m128", P),
               ("negm", GRID_W), ("cos", TS), ("sin", TS), ("iota", SLS), ("gmask", NPAIR * NE),
               ("gmaskp", 2 * NE), ("pm64", 1), ("pm16", 1), ("eps", 1)]:
    CST[_n] = (_at, _w)
    _at += _w
CSTW = _at


def constants():
    c = np.zeros((P, CSTW), np.float32)

    def put(name, a):
        o, w = CST[name]
        c[:, o:o + w] = a.reshape(P, w)

    i, j = np.arange(P)[:, None], np.arange(P)[None, :]
    put("ident", np.eye(P))
    put("tri", np.concatenate([i >= j, i <= j], 1) * 1.0)
    put("strict", np.concatenate([i > j, i < j], 1) * 1.0)
    put("blk16", (i // 16 == j // 16) * 1.0)
    for b in (32, 64, 128):
        put(f"m{b}", ((i // b == j // b) & (i // (b // 2) != j // (b // 2))) * 1.0)
    col = np.arange(P)[:, None] % GRID_W
    cs = np.clip(col - WIN_C // 2, 0, GRID_W - WIN_C)
    w = np.arange(GRID_W)[None, :]
    put("negm", np.where((w >= cs) & (w < cs + WIN_C), 0.0, NEG))
    quarter = 16
    inv = (1.0 / (np.float32(10000.0) ** (np.arange(quarter, dtype=np.float32) / np.float32(quarter)))).astype(np.float32)
    t = np.arange(TS)
    pos = np.stack([t // GRID_W, t % GRID_W]).astype(np.float32)
    p = np.arange(P) % 64
    ang = (pos[p // 32, :] * inv[p % quarter][:, None]).astype(np.float32)
    sign = np.where((p // quarter) % 2 == 0, -1.0, 1.0)[:, None]
    put("cos", np.cos(ang))
    put("sin", np.sin(ang) * sign)
    put("iota", np.broadcast_to(np.arange(SLS), (P, SLS)))
    e = np.arange(NE)[None, None, :]
    put("gmask", (e == 2 * np.arange(NPAIR)[None, :, None] + (np.arange(P) // SLS)[:, None, None]) * 1.0)
    put("gmaskp", (e == 8 * np.arange(2)[None, :, None] + (np.arange(P) // SLP)[:, None, None]) * 1.0)
    put("pm64", (np.arange(P) % SLS)[:, None])
    put("pm16", (np.arange(P) % SLP)[:, None])
    put("eps", np.full((P, 1), EPS))
    return c


GROUPS = [(0, 0), (1, 3), (0, 1), (1, 2), (0, 2), (1, 1), (0, 3), (1, 0), (0, 4), (1, 4)]
NG = len(GROUPS)
ADDS = [g in ((0, 2), (1, 1), (0, 3), (1, 0), (1, 4)) for g in GROUPS]
AUNITS = [(h, qt) for h in range(H) for qt in range(NT)]
NA = len(AUNITS)


class Signals(dict):

    def __init__(self, nc, ctx):
        super().__init__()
        self.nc, self.ctx = nc, ctx

    def __missing__(self, name):
        self[name] = self.ctx.enter_context(self.nc.semaphore(name))
        return self[name]


class Chain:

    def __init__(self, eng, sem):
        self.eng, self.sem, self.n = eng, sem, 0

    def mark(self, ins):
        ins.then_inc(self.sem, 1)
        self.n += 1

    def wait(self):
        self.eng.wait_ge(self.sem, self.n)

    def link(self, ins):
        self.mark(ins)
        self.wait()


def build(nc, A, O):
    with ExitStack() as ctx:
        sig = Signals(nc, ctx)

        def sb(name, words):
            return ctx.enter_context(nc.sbuf_tensor(name, [P, words], F32))

        xT = sb("xT", KD * T)[:, :].rearrange("p (k t) -> p k t", k=KD)
        hT = sb("hT", KD * T)[:, :].rearrange("p (k t) -> p k t", k=KD)
        ring = sb("ring", RING * 4096)[:, :].rearrange("p (s w) -> p s w", s=RING)
        cst = sb("cst", CSTW)
        ones = sb("ones", P)
        vcol = sb("vcol", V_ROWS)
        vrow = sb("vrow", P)
        ccol = sb("ccol", 24)
        mod = sb("mod", 96)[:, :].rearrange("p (m g) -> p m g", g=2)
        amod = sb("amod", 32)[:, :].rearrange("p (n k g) -> p n k g", n=2, k=KD)
        small = sb("small", 528)
        al, dtb = small[:, 0:8], small[:, 8:16]
        lq = small[:, 16:272]
        wab = small[:, 272:400].rearrange("p (k c) -> p k c", k=KD)
        wrt = small[:, 400:528].rearrange("p (k c) -> p k c", k=KD)
        sc = sb("sc", 256)
        arena = sb("arena", 26880)

        def C(name):
            o, w = CST[name]
            return cst[:, o:o + w]

        ident = C("ident")

        def at(off, shape):
            n = int(np.prod(shape))
            v = arena[:, off:off + n]
            if len(shape) == 2:
                v = v.rearrange("p (a b) -> p a b", a=shape[0])
            if len(shape) == 3:
                v = v.rearrange("p (a b c) -> p a b c", a=shape[0], b=shape[1])
            return v

        obT, oaT, ocT = at(0, (H, T)), at(2560, (H, T)), at(5120, (H, T))
        cT = [at(2560 + 2560 * i, (H, T)) for i in range(3)]
        ktok, vtok = at(10240, (NT, BR)), at(12800, (NT, BR))
        otok = at(7680, (NT, BR))
        state = [at(15360 + 512 * i, (H, P)) for i in range(4)]
        pre = at(17408, (2 * H, PADW))
        cvt = at(22592, (2, T + 4))
        NS = 23880
        sqb, rt = at(NS, (2, T)), at(NS + 2 * T, (2, T))
        (gE, gL, gA, gLT, gAT, gD, gDT, gD2, gD2T, gD4, gD4T, gX, c32, c64, c128, gVB, gKB, gKD) = [
            at(17408 + 512 * i, (H, P)) for i in range(18)]
        aQ, aK, aV = at(7680, (H, T)), at(10240, (H, T)), at(12800, (NT, BR))
        ctok = [at(15360 + 1024 * i, (H, P)) for i in range(2)]
        cval = [at(15872 + 1024 * i, (H, P)) for i in range(2)]
        ckT = at(17408, (H, P))
        prob = at(17920, (2, T))
        comb = at(19200, (T,))
        aT = at(19840, (NT, TS))
        bmt = at(22400, (2, TS))
        rot = at(23424, (TS,))
        ktp = at(25216, (BR,))
        sq1, rt1 = at(23936, (T,)), at(24576, (T,))
        merged = at(7680, (KD, T))
        gsig = at(12800, (4, T))
        brs, brsp = at(15360, (2, TS)), at(16384, (H, TP))
        xtmp, xtmpp = at(0, (2, TS)), at(2 * TS, (H, TP))
        XE = at(0, (NE, KD, SL))
        yTp = at(10240, (KD, NE * SLP))
        yTs = at(12288, (KD, P))
        hgate, hup = at(13312, (2, 4 * SL)), at(13952, (2, 4 * SL))
        hid = at(14592, (2, KD * SL))
        h2tok = at(15872, (NT, D))
        oneh = at(20992, (NTS, NE * SLS))
        onehp = at(25088, (NE * SLP,))
        aff = at(25344, (NT, NE))
        affs = at(25424, (NT, NE))
        post = at(25504, (NT, NE))
        affT, msk = at(25584, (T,)), at(26224, (T,))
        posm = at(0, (T,))
        onesr = at(640, (T,))
        sel, selp = at(1280, (NE * SLS,)), at(1280 + NE * SLS, (NE * SLP,))
        Ysc = at(15872, (NPAIR, D))
        YP = at(24064, (2, D))
        ST = hT[:, 0:7, :].rearrange("p k t -> p (k t)")[:, 0:NPAIR * TS].rearrange("p (j t) -> p j t", j=NPAIR)
        STP = hT[:, 7, 0:2 * TP].rearrange("p (j t) -> p j t", j=2)
        gsl = small[:, 0:NPAIR]
        gslp = small[:, NPAIR:NPAIR + 2]
        xtok = at(0, (NT, D))
        crow = at(5120, (P,))
        ytok = at(0, (2, D))

        ps = [ctx.enter_context(nc.psum_tensor(f"unit{i}", [P, 512], F32)) for i in range(2)]
        W = [ctx.enter_context(nc.psum_tensor(f"work{i}", [P, 512], F32)) for i in range(6)]

        scr = nc.dram_tensor("rpb_scratch", [DEPTH, H * (2 * WIN_R - 1), GRID_W * (2 * GRID_W - 1)], F32).ap()
        RPW = 2 * GRID_W - 1
        rpt = vrow[0:H * (2 * WIN_R - 1), 0:RPW]

        def h4(ap):
            return ap[:, :].rearrange("p (h c) -> p h c", h=H)

        def tile_t(t):
            return slice(t * P, (t + 1) * P)

        GRP = ((0, slice(0, TS)), (1, slice(TS, T)))

        nega = sc[:, 0:8]
        gg = sc[:, 8:48].rearrange("p (t c) -> p t c", t=NT)
        beta = sc[:, 48:88].rearrange("p (t c) -> p t c", t=NT)
        gt1_, gt2_ = sc[:, 88:128].rearrange("p (t c) -> p t c", t=NT), sc[:, 128:168].rearrange("p (t c) -> p t c", t=NT)
        gcum, glast, eg, egl, kds, bexp, gdif = [sc[:, 168 + 4 * i:172 + 4 * i] for i in range(7)]
        lamc = sc[:, 196:197]
        lam4 = sc[:, 197:201]
        mx, rs, cf = sc[:, 204:208], sc[:, 208:212], sc[:, 212:216]
        nm = sc[:, 216:218]
        orms = sc[:, 220:240]
        sof = sc[:, 240:245]
        top8 = sc[:, 248:256]

        block = ctx.enter_context(nc.Block())

        @block.sync
        def _(sp):
            def slot_free(c):
                if c >= RING:
                    sp.wait_ge(sig["unit_computed"], units_through(c - RING))

            def load(c, src, words=4096):
                slot_free(c)
                sp.dma_start(ring[:, c % RING, 0:words].rearrange("p (k n) -> p k n", n=512), src)\
                    .then_inc(sig[f"chunk{c % RING}_loaded"], 16)

            for l in range(DEPTH):
                win = A["w_in"][l].rearrange("(k p) n -> p k n", p=P)
                for name, i in PLAN:
                    c = chunk_no(l, name, i)
                    if name == "ada":
                        load(c, A["w_ada"][l].rearrange("(k p) n -> p k n", p=P)[:, :, 512 * i:512 * i + 512])
                    elif name == "wo":
                        load(c, A["w_out"][l].rearrange("(k p) n -> p k n", p=P)[:, :, 512 * i:512 * i + 512])
                    elif name.startswith("br"):
                        load(c, A["w_br_" + name[2]][l].rearrange("(k p) n -> p k n", p=P)[:, :, 512 * i:512 * i + 512],
                             2048)
                    else:
                        load(c, win[:, :, SEG[name] + 512 * i:SEG[name] + 512 * i + 512])
                ub = unit_no(l, "pair")
                sp.wait_ge(sig["unit_computed"], ub)
                with sp.Fori(0, NPAIR) as j:
                    for q in range(PAIR_CHUNKS):
                        e, part = 2 * j + q // 6, q % 6
                        w = A[("w_e_gate", "w_e_up", "w_e_gate", "w_e_up", "w_e_down", "w_e_down")[part]][l]
                        half = (0, 0, 1, 1, 0, 1)[part]
                        src = w[bass.ds(e, 1), :, 512 * half:512 * half + 512].rearrange("o (k p) n -> p (o k) n", p=P)
                        back = q - RING if q >= RING else q - RING + PAIR_CHUNKS - PAIR_UNITS
                        sp.wait_ge(sig["unit_computed"], j * PAIR_UNITS + (ub + back + 1))
                        sp.dma_start(ring[:, q % RING, :].rearrange("p (k n) -> p k n", n=512), src)\
                            .then_inc(sig[f"chunk{q % RING}_loaded"], 16)

        @block.gpsimd
        def _(pool):
            pool.dma_start(cst[:, :], A["consts"]).then_inc(sig["consts_loaded"], 16)
            for i, n in enumerate(("c", "c_ctx", "g_final")):
                src = A[n][0] if n == "c" else A[n]
                pool.dma_start(crow[8 * i:8 * i + 8, :], src.rearrange("(k p) -> k p", p=P))\
                    .then_inc(sig["cond_loaded"], 16)
            for l in range(DEPTH):
                if l:
                    pool.wait_ge(sig["x_added"], l * 20)
                rows = [(V_BADA, 48, A["b_ada"][l].rearrange("(m p) -> m p", p=P)),
                        (V_G1, 8, A["g_norm1"][l].rearrange("(m p) -> m p", p=P)),
                        (V_G2, 8, A["g_norm2"][l].rearrange("(m p) -> m p", p=P)),
                        (V_GO, 1, A["g_onorm"][l:l + 1, :]), (V_GS, 1, A["g_subln"][l:l + 1, :])]
                for r, n, src in rows:
                    pool.dma_start(vrow[r:r + n, :], src).then_inc(sig["vectors_loaded"], 16)
                for j in range(CONV):
                    pool.dma_start(vrow[V_CONV + 12 * j:V_CONV + 12 * j + 12, :],
                                   A["conv_w"][l, j].rearrange("(c p) -> c p", p=P)).then_inc(sig["vectors_loaded"], 16)
                pool.dma_start(al, A["a_log"][l].rearrange("d h -> (d h)").partition_broadcast(P))\
                    .then_inc(sig["small_loaded"], 16)
                pool.dma_start(dtb, A["dt_bias"][l].rearrange("d h -> (d h)").partition_broadcast(P))\
                    .then_inc(sig["small_loaded"], 16)
                pool.dma_start(lq, A["lam_qk"][l].rearrange("a d -> (a d)").partition_broadcast(P))\
                    .then_inc(sig["small_loaded"], 16)
                pool.dma_start(wab, A["w_in"][l].rearrange("(k p) n -> p k n", p=P)[:, :, SEG["ab"]:SEG["ab"] + 16])\
                    .then_inc(sig["small_loaded"], 16)
                pool.dma_start(wrt, A["w_router"][l].rearrange("(k p) n -> p k n", p=P)).then_inc(sig["small_loaded"], 16)
                for d in range(2):
                    pool.dma_start(state[d], A["state_delta"][0, l, d].rearrange("h k v -> k h v"))\
                        .then_inc(sig["state_loaded"], 16)
                pool.wait_ge(sig["vectors_turned"], l + 1)
                pool.memset(rpt, 0.0).then_inc(sig["rpb_cleared"], 1)
                pool.wait_ge(sig["rpb_cleared"], l + 1)
                pool.dma_start(rpt[:, GRID_W - WIN_C:GRID_W + WIN_C - 1], A["rpb"][l].rearrange("h a b -> (h a) b"))\
                    .then_inc(sig["rpb_loaded"], 16)
                pool.wait_ge(sig["rpb_loaded"], 16 * (l + 1))
                pool.dma_start(scr[l].rearrange("r (c x) -> r c x", c=GRID_W),
                               rpt.unsqueeze(1).to_broadcast([H * (2 * WIN_R - 1), GRID_W, RPW]))\
                    .then_inc(sig["rpb_padded"], 16)
                pool.wait_ge(sig["delta_turned"], H * (l + 1))
                pool.wait_ge(sig["state_stored"], 32 * (l + 1))
                for i, (kk, vv) in enumerate((("cache_diff_k", "cache_diff_v"), ("cache_na_k", "cache_na_v"))):
                    pool.dma_start(ctok[i], A[kk][0, l]).then_inc(sig["cache_loaded"], 16)
                    pool.dma_start(cval[i], A[vv][0, l]).then_inc(sig["cache_loaded"], 16)
                pool.wait_ge(sig["rpb_padded"], 16 * (l + 1))
                n = 0
                for h in range(H):
                    for qt in range(NTS):
                        m = l * H * NTS + n
                        b = bmt[:, n % 2, :]
                        if n >= 2:
                            pool.wait_ge(sig["bias_used"], m - 1)
                        for rr in range(P // GRID_W):
                            r = qt * (P // GRID_W) + rr
                            off = ((l * H + h) * (2 * WIN_R - 1) + WIN_R - 1 - r) * GRID_W * RPW + GRID_W - 1
                            src = bass.AP(scr.tensor, off, [[RPW - 1, GRID_W], [GRID_W * RPW, GROWS], [1, GRID_W]])
                            pool.dma_start(b[rr * GRID_W:(rr + 1) * GRID_W, :]
                                           .rearrange("p (i w) -> p i w", i=GROWS), src)\
                                .then_inc(sig[f"bias{n % 2}_loaded"], 16)
                        pool.wait_ge(sig[f"bias{n % 2}_loaded"], 32 * (l * H * NTS // 2 + n // 2 + 1))
                        b3 = b.rearrange("p (i w) -> p i w", i=GROWS)
                        pool.tensor_tensor(b3, b3, C("negm").unsqueeze(1).to_broadcast([P, GROWS, GRID_W]), ALU.add)\
                            .then_inc(sig["bias_ready"], 1)
                        n += 1

        @block.tensor
        def _(pe):
            mm = nc.tensor.matmul
            tr = nc.tensor.transpose
            unit = [0]

            def begin(n):
                if n >= 2:
                    pe.wait_ge(sig["unit_emptied"], n - 1)
                return ps[n % 2]

            def chunk_in(c):
                pe.wait_ge(sig[f"chunk{c % RING}_loaded"], 16 * (c // RING + 1))
                return ring[:, c % RING, :].rearrange("p (k n) -> p k n", n=512)

            def used(ins):
                ins.then_inc(sig["unit_computed"], 1)

            def project(l, name, i, src, kk=KD, wait=None):
                c = chunk_no(l, name, i)
                w = chunk_in(c)
                bank = begin(unit_no(l, name, i))
                for m in range(4):
                    for k in range(kk):
                        if wait and m == 0:
                            pe.wait_ge(*wait(k))
                        last = mm(bank[:, tile_t(m)], w[:, k, m * P:(m + 1) * P], src[:, k, TS:T],
                                  start=k == 0, stop=k == kk - 1)
                used(last)
                for m in range(4):
                    bank = begin(unit_no(l, name, i, 1 + m))
                    for k in range(kk):
                        last = mm(bank[:, :], w[:, k, m * P:(m + 1) * P], src[:, k, 0:TS],
                                  start=k == 0, stop=k == kk - 1)
                    used(last)

            def project_t(l, name):
                w = chunk_in(chunk_no(l, name))
                for t in range(NT):
                    big = begin(unit_no(l, name, 0, t))
                    for k in range(KD):
                        last = mm(big[:, :], hT[:, k, tile_t(t)], w[:, k, :], start=k == 0, stop=k == KD - 1)
                    used(last)

            def ada(l, a):
                w = chunk_in(chunk_no(l, "ada", a))
                big = begin(unit_no(l, "ada", a))
                cond = ccol[:, 0:16].rearrange("p (g k) -> p k g", g=2)
                for m in range(4):
                    for k in range(KD):
                        last = mm(big[:, 2 * m:2 * m + 2], w[:, k, m * P:(m + 1) * P], cond[:, k, :],
                                  start=k == 0, stop=k == KD - 1)
                used(last)

            def norm_sums(n):
                for k in range(KD):
                    pe.wait_ge(sig["squared"], n * KD + k + 1)
                    mm(W[0][:, :], ones[:, :], sqb[:, k % 2, 0:TS], start=k == 0, stop=k == KD - 1)
                    mm(W[1][:, 0:TP], ones[:, :], sqb[:, k % 2, TS:T], start=k == 0, stop=k == KD - 1)\
                        .then_inc(sig["square_summed"], 1)

            pe.wait_ge(sig["consts_loaded"], 16)
            pe.wait_ge(sig["x_loaded"], 32)
            for k in range(KD):
                big = begin(k)
                for t in range(NTS):
                    last = tr(big[:, tile_t(t)], xtok[:, t, tile_t(k)], ident)
                used(last)
            for half in range(2):
                big = begin(KD + half)
                for k in range(4):
                    last = tr(big[:, tile_t(k)], xtok[:, NTS, tile_t(4 * half + k)], ident)
                used(last)
            pe.wait_ge(sig["cond_silu"], 1)
            pe.wait_ge(sig["cond_loaded"], 48)
            tr(W[0][:, 0:24], crow[0:24, :], ident[0:24, 0:24]).then_inc(sig["cond_turned"], 1)
            pe.wait_ge(sig["cond_ready"], 1)
            pe.wait_ge(sig["ones_ready"], 1)

            for l in range(DEPTH):
                pe.wait_ge(sig["vectors_loaded"], 160 * (l + 1))
                tr(W[2][:, 0:V_ROWS], vrow[0:V_ROWS, :], ident[0:V_ROWS, 0:V_ROWS]).then_inc(sig["vectors_turned"], 1)
                for a in range(4):
                    ada(l, a)
                norm_sums(2 * l)
                for i, s in enumerate(("qb", "kb", "vb", "zb")):
                    project(l, s, 0, hT, wait=(lambda k: (sig["h_ready"], 2 * l * KD + k + 1)) if i == 0 else None)
                    ada(l, 4 + i)
                pe.wait_ge(sig["small_loaded"], 80 * (l + 1))
                for t in range(NT):
                    for k in range(KD):
                        last = mm(W[4][:, 16 * t:16 * t + 16], hT[:, k, tile_t(t)], wab[:, k, :],
                                  start=k == 0, stop=k == KD - 1)
                last.then_inc(sig["ab_computed"], 1)
                for j in range(2 * H):
                    n = 2 * H * l + j
                    pe.wait_ge(sig["qk_squared"], n + 1)
                    if j >= 2:
                        pe.wait_ge(sig["qk_rooted"], n - 1)
                    mm(W[2 * (j % 2)][:, :], ones[:, :], sqb[:, j % 2, 0:TS], start=True, stop=True)
                    mm(W[2 * (j % 2) + 1][:, 0:TP], ones[:, :], sqb[:, j % 2, TS:T], start=True, stop=True)\
                        .then_inc(sig["qk_summed"], 1)
                pe.wait_ge(sig["qk_scaled"], 2 * H * (l + 1))
                pe.wait_ge(sig["conv_silu"], 12 * (l + 1))
                for t in range(NT):
                    n = NT * l + t
                    if t >= 1:
                        pe.wait_ge(sig["ktok_ready"], n)
                        pe.wait_ge(sig["vtok_ready"], n)
                    for h in range(H):
                        tr(W[0][:, tile_t(h)], cT[1][:, h, tile_t(t)], ident)
                    for h in range(H):
                        last = tr(W[1][:, tile_t(h)], cT[2][:, h, tile_t(t)], ident)
                    last.then_inc(sig["kv_turned"], 1)
                pe.wait_ge(sig["ktok_ready"], NT * (l + 1))
                pe.wait_ge(sig["vtok_ready"], NT * (l + 1))
                pe.wait_ge(sig["g_ready"], l + 1)
                for i, (d, t) in enumerate(GROUPS):
                    n = NG * l + i
                    st = state[d + (2 if t == NTS else 0)]
                    cum = C("tri")[:, (1 - d) * P:(2 - d) * P]
                    if i:
                        pe.wait_ge(sig["state_updated"], n)
                    for h in range(H):
                        mm(W[0][:, tile_t(h)], gg[:, t, 4 * d + h:4 * d + h + 1].to_broadcast([P, P]), cum,
                           start=True, stop=True)
                    mm(W[3][:, 0:4], cum, gg[:, t, 4 * d:4 * d + 4], start=True, stop=True)\
                        .then_inc(sig["gsum_computed"], 1)
                    for h in range(H):
                        mm(W[1][:, tile_t(h)], cT[1][:, h, tile_t(t)], cT[1][:, h, tile_t(t)], start=True, stop=True)
                    for h in range(H):
                        last = mm(W[2][:, tile_t(h)], cT[0][:, h, tile_t(t)], cT[1][:, h, tile_t(t)],
                                  start=True, stop=True)
                    last.then_inc(sig["kk_computed"], 1)
                    pe.wait_ge(sig["la_ready"], n + 1)
                    for h in range(H):
                        tr(W[0][:, tile_t(h)], gL[:, h, :], ident)
                    for h in range(H):
                        last = tr(W[3][:, tile_t(h)], gA[:, h, :], ident)
                    last.then_inc(sig["la_turned"], 1)
                    pe.wait_ge(sig["d_ready"], n + 1)
                    for h in range(H):
                        mm(W[1][:, tile_t(h)], gDT[:, h, :], gD[:, h, :], start=True, stop=True)
                    for h in range(H):
                        last = mm(W[2][:, tile_t(h)], gD[:, h, :], gDT[:, h, :], start=True, stop=True)
                    last.then_inc(sig["d2_computed"], 1)
                    pe.wait_ge(sig["d2_ready"], n + 1)
                    pe.wait_ge(sig["d2t_ready"], n + 1)
                    for h in range(H):
                        mm(W[4][:, tile_t(h)], gD2T[:, h, :], gX[:, h, :], start=True, stop=True)
                    for h in range(H):
                        mm(W[1][:, tile_t(h)], gD2T[:, h, :], gD2[:, h, :], start=True, stop=True)
                    for h in range(H):
                        last = mm(W[2][:, tile_t(h)], gD2[:, h, :], gD2T[:, h, :], start=True, stop=True)
                    last.then_inc(sig["d4_computed"], 1)
                    pe.wait_ge(sig["d4_ready"], n + 1)
                    pe.wait_ge(sig["x1_ready"], n + 1)
                    for h in range(H):
                        mm(W[1][:, tile_t(h)], gD4[:, h, :], gD4T[:, h, :], start=True, stop=True)
                    for h in range(H):
                        last = mm(W[2][:, tile_t(h)], gD4T[:, h, :], gX[:, h, :], start=True, stop=True)
                    last.then_inc(sig["d8_computed"], 1)
                    pe.wait_ge(sig["d8t_ready"], n + 1)
                    pe.wait_ge(sig["x2_ready"], n + 1)
                    for h in range(H):
                        last = mm(W[4][:, tile_t(h)], gD2T[:, h, :], gX[:, h, :], start=True, stop=True)
                    last.then_inc(sig["x3_computed"], 1)
                    pe.wait_ge(sig["x3_ready"], n + 1)
                    for h in range(H):
                        last = tr(W[1][:, tile_t(h)], gX[:, h, :], ident)
                    last.then_inc(sig["x3_turned"], 1)
                    for s, cm in enumerate((c32, c64, c128)):
                        m = 3 * n + s
                        pe.wait_ge(sig["s_ready"], m + 1)
                        for h in range(H):
                            last = mm(W[2][:, tile_t(h)], cm[:, h, :], gX[:, h, :], start=True, stop=True)
                        last.then_inc(sig["ct_computed"], 1)
                        pe.wait_ge(sig["y_ready"], m + 1)
                        for h in range(H):
                            last = mm(W[4][:, tile_t(h)], gD2[:, h, :], gD[:, h, :], start=True, stop=True)
                        if s < 2:
                            for h in range(H):
                                last = mm(W[1][:, tile_t(h)], gD[:, h, :], gD2[:, h, :], start=True, stop=True)
                        last.then_inc(sig["tct_computed"], 1)
                    pe.wait_ge(sig["inverse_ready"], n + 1)
                    for h in range(H):
                        last = mm(W[1][:, tile_t(h)], gKB[:, h, :], gD[:, h, :], start=True, stop=True)
                    last.then_inc(sig["w_computed"], 1)
                    if i == 0:
                        pe.wait_ge(sig["state_loaded"], 32 * (l + 1))
                    if i == 0:
                        pe.wait_ge(sig["state_zeroed"], l + 1)
                    for h in range(H):
                        last = mm(W[2][:, tile_t(h)], cT[0][:, h, tile_t(t)], st[:, h, :], start=True, stop=True)
                    last.then_inc(sig["qs_computed"], 1)
                    pe.wait_ge(sig["w_ready"], n + 1)
                    for h in range(H):
                        mm(W[0][:, tile_t(h)], gD[:, h, :], gVB[:, h, :], start=True, stop=False)
                        last = mm(W[0][:, tile_t(h)], gDT[:, h, :], st[:, h, :], start=False, stop=True)
                    last.then_inc(sig["vnew_computed"], 1)
                    pe.wait_ge(sig["vnew_ready"], n + 1)
                    for h in range(H):
                        mm(W[3][:, tile_t(h)], gAT[:, h, :], gD4[:, h, :], start=True, stop=True)
                    for h in range(H):
                        last = mm(W[4][:, tile_t(h)], gKD[:, h, :], gD4[:, h, :], start=True, stop=True)
                    last.then_inc(sig["av_computed"], 1)
                pe.wait_ge(sig["otok_ready"], l + 1)
                for h in range(H):
                    if h:
                        pe.wait_ge(sig["delta_turned"], H * l + h)
                    for t in range(NTS):
                        tr(W[0][:, tile_t(t)], otok[:, t, tile_t(h)], ident)
                    tr(W[1][:, 0:TP], otok[:, NTS, tile_t(h)], ident).then_inc(sig["o_turned"], 1)

                for br in range(2):
                    names = ("qa", "ka", "va") if br == 0 else ("qc", "kc", "vc")
                    if br == 0:
                        project(l, "qa", 0, hT)
                        ada(l, 8)
                        project(l, "ka", 0, hT)
                        ada(l, 9)
                        project_t(l, "va")
                        ada(l, 10)
                    else:
                        project(l, "qc", 0, hT)
                        ada(l, 11)
                        project(l, "kc", 0, hT)
                        project_t(l, "vc")
                    nb = 2 * l + br
                    pe.wait_ge(sig["cache_loaded"], 64 * (l + 1))
                    for h in range(H):
                        tr(W[3][:, tile_t(h)], ctok[br][:, h, :], ident)
                    pe.wait_ge(sig["unit_emptied"], unit_no(l, names[1], 0, 5))
                    for h in range(H):
                        last = tr(W[4][:, tile_t(h)], aK[:, h, TS:T], ident)
                    last.then_inc(sig["keys_turned"], 1)
                    pe.wait_ge(sig["keys_ready"], nb + 1)
                    pe.wait_ge(sig["new_k_copied"], nb + 1)
                    if br == 0:
                        pe.wait_ge(sig["rotated"], 2 * H * (l + 1))
                    pe.wait_ge(sig["unit_emptied"], unit_no(l, names[2], 0, NT))
                    for i, (h, qt) in enumerate(AUNITS):
                        n = NA * nb + i
                        comps = 2 if br == 0 else 1
                        kd = P // comps
                        if n:
                            pe.wait_ge(sig["probs_ready"], n)
                        for c in range(comps):
                            rows = slice(c * kd, (c + 1) * kd)
                            q = aQ[rows, h, tile_t(qt)]
                            if qt < NTS:
                                mm(W[c][:, :], q, aK[rows, h, 0:TS], start=True, stop=True)
                                last = mm(W[2 + 3 * c][:, 0:P], q, ckT[rows, h, :], start=True, stop=True)
                            else:
                                last = mm(W[2 + 3 * c][:, 0:P], q, aK[rows, h, TS:T], start=True, stop=True)
                        last.then_inc(sig["scores_computed"], 1)
                        pe.wait_ge(sig["probs_ready"], n + 1)
                        if i:
                            pe.wait_ge(sig["probs_copied"], n)
                        if qt < NTS:
                            for kt in range(NTS):
                                tr(W[3][:, tile_t(kt)], comb[:, tile_t(kt)], ident)
                            tr(W[4][:, 0:P], comb[:, TS:T], ident).then_inc(sig["probs_turned"], 1)
                        else:
                            tr(W[4][:, 0:P], comb[:, TS:T], ident).then_inc(sig["probs_turned"], 1)
                        if qt == NTS - 1:
                            m = 2 * (H * nb + h)
                            pe.wait_ge(sig["probs_copied"], n + 1)
                            if m:
                                pe.wait_ge(sig["attn_out"], m)
                            for kt in range(NT):
                                v = aV[:, kt, tile_t(h)] if kt < NTS else cval[br][:, h, :]
                                last = mm(W[0][:, :], v, aT[:, kt, :], start=kt == 0, stop=kt == NT - 1)
                            last.then_inc(sig["pv_computed"], 1)
                            if br == 0:
                                pe.wait_ge(sig["sub_squared"], 2 * (H * l + h) + 1)
                                mm(W[1][:, :], ones[:, :], sq1[:, 0:TS], start=True, stop=True)\
                                    .then_inc(sig["sub_summed"], 1)
                            pe.wait_ge(sig["attn_out"], m + 1)
                        if qt == NTS:
                            m = 2 * (H * nb + h) + 1
                            pe.wait_ge(sig["probs_copied"], n + 1)
                            mm(W[0][:, 0:P], aV[:, NTS, tile_t(h)], aT[:, NTS, 0:P], start=True, stop=True)\
                                .then_inc(sig["pv_computed"], 1)
                            if br == 0:
                                pe.wait_ge(sig["sub_squared"], 2 * (H * l + h) + 2)
                                mm(W[1][:, 0:P], ones[:, :], sq1[:, TS:T], start=True, stop=True)\
                                    .then_inc(sig["sub_summed"], 1)
                            pe.wait_ge(sig["attn_out"], m + 1)

                for b, (s, src) in enumerate((("a", oaT), ("b", obT), ("c", ocT))):
                    for half in range(2):
                        project(l, "g" + s, half, hT)
                        project(l, "br" + s, half, src, kk=H)
                for half in range(2):
                    project(l, "wo", half, merged,
                            wait=(lambda k: (sig["merged_ready"], 30 * (l + 1))) if half == 0 else None)
                norm_sums(2 * l + 1)
                pe.wait_ge(sig["h_ready"], (2 * l + 2) * KD)
                for t in range(NT):
                    for k in range(KD):
                        last = mm(W[0][:, NE * t:NE * t + NE], hT[:, k, tile_t(t)], wrt[:, k, :],
                                  start=k == 0, stop=k == KD - 1)
                last.then_inc(sig["logits_computed"], 1)
                for t in range(NT):
                    for half in range(2):
                        n = 2 * NT * l + 2 * t + half
                        if n >= 2:
                            pe.wait_ge(sig["h2_copied"], n - 1)
                        for k in range(4):
                            last = tr(W[1 + half][:, tile_t(k)], hT[:, 4 * half + k, tile_t(t)], ident)
                        last.then_inc(sig["h2_turned"], 1)
                pe.wait_ge(sig["aff_ready"], l + 1)
                for t in range(NTS):
                    tr(W[3][0:NE, tile_t(t)], aff[:, t, :], ident)
                tr(W[4][0:NE, 0:TP], aff[:, NTS, :], ident).then_inc(sig["aff_turned"], 1)
                pe.wait_ge(sig["slots_ready"], l + 1)
                for t in range(NT):
                    last = tr(W[0][:, NE * t:NE * t + NE], posm[0:NE, tile_t(t)], ident[0:NE, 0:NE])
                last.then_inc(sig["slots_turned"], 1)
                pe.wait_ge(sig["h2_copied"], 2 * NT * (l + 1))
                for j in range(NPAIR + 2):
                    n = (NPAIR + 2) * l + j
                    if j >= 2:
                        pe.wait_ge(sig["spread_ready"], n - 1)
                    if j < NPAIR:
                        last = mm(W[1 + j % 2][:, :], sel[0:NE, tile_t(j)], posm[0:NE, 0:TS], start=True, stop=True)
                    else:
                        g = j - NPAIR
                        last = mm(W[1 + j % 2][:, 0:TP], selp[0:NE, tile_t(g)], posm[0:NE, TS:T], start=True, stop=True)
                    last.then_inc(sig["spread_computed"], 1)
                pe.wait_ge(sig["onehot_ready"], l + 1)
                for j in range(NPAIR):
                    for t in range(NTS):
                        mm(W[3][:, NE * j:NE * j + NE], oneh[:, t, tile_t(j)], aff[:, t, :],
                           start=t == 0, stop=t == NTS - 1)
                for g in range(2):
                    last = mm(W[4][:, NE * g:NE * g + NE], onehp[:, tile_t(g)], aff[:, NTS, :], start=True, stop=True)
                last.then_inc(sig["slotgate_computed"], 1)
                pe.wait_ge(sig["spread_ready"], (NPAIR + 2) * (l + 1))
                pe.wait_ge(sig["slotgate_ready"], l + 1)
                for i in range(3 * KD):
                    n = 3 * KD * l + i
                    k, part = i // 3, i % 3
                    wb = W[i % 4]
                    if i >= 4:
                        pe.wait_ge(sig["gathered"], n - 3)
                    if part < 2:
                        for t in range(NTS):
                            last = mm(wb[:, :], h2tok[:, t, tile_t(k)], oneh[:, t, part * 512:part * 512 + 512],
                                      start=t == 0, stop=t == NTS - 1)
                    else:
                        last = mm(wb[:, 0:NE * SLP], h2tok[:, NTS, tile_t(k)], onehp, start=True, stop=True)
                    last.then_inc(sig["gather_computed"], 1)
                pe.wait_ge(sig["gathered"], 3 * KD * (l + 1))
                cb, ub = l * LAYER_CHUNKS + PRE_CHUNKS, unit_no(l, "pair")
                with pe.Fori(0, NPAIR) as j:
                    def loop_begin(q):
                        pe.wait_ge(sig["unit_emptied"], j * PAIR_UNITS + (ub + q - 1))
                        return ps[(ub + q) % 2]

                    def loop_chunk(q):
                        pe.wait_ge(sig[f"chunk{q % RING}_loaded"],
                                   j * (16 * PAIR_CHUNKS // RING) + 16 * ((cb + q) // RING + 1))
                        return ring[:, q % RING, :].rearrange("p (k n) -> p k n", n=512)

                    for x in range(2):
                        for part in range(6):
                            q = 6 * x + part
                            w = loop_chunk(q)
                            big = loop_begin(q)
                            if part == 4:
                                pe.wait_ge(sig["hidden_ready"], j * 4 + (NE * 2 * l + 2 * x + 4))
                            for m in range(4):
                                for k in range(KD):
                                    rhs = XE[:, bass.ds(2 * j + x, 1), k, :] if part < 4 else \
                                        hid[:, x, k * SL:(k + 1) * SL]
                                    last = mm(big[:, m * SL:(m + 1) * SL], w[:, k, m * P:(m + 1) * P], rhs,
                                              start=k == 0, stop=k == KD - 1)
                            used(last)
                    for half in range(2):
                        q = 12 + half
                        big = loop_begin(q)
                        if half == 0:
                            pe.wait_ge(sig["unit_emptied"], j * PAIR_UNITS + (ub + 12))
                        for k in range(4):
                            last = tr(big[:, tile_t(k)], yTs[:, 4 * half + k, :], ident)
                        used(last)
                for g in range(2):
                    for half in range(2):
                        n = unit_no(l, "yp", 0, 2 * g + half)
                        big = begin(n)
                        for k in range(4):
                            last = tr(big[:, tile_t(k)], yTp[:, 4 * half + k, tile_t(g)], ident)
                        used(last)
                pe.wait_ge(sig["yp_gated"], l + 1)
                for half in range(2):
                    big = begin(unit_no(l, "scatter", 0, 5 * half))
                    for k in range(4):
                        for g in range(2):
                            last = mm(big[:, tile_t(k)], YP[:, g, tile_t(4 * half + k)], STP[:, g, :],
                                      start=g == 0, stop=g == 1)
                    used(last)
                    for k in range(4):
                        big = begin(unit_no(l, "scatter", 0, 5 * half + 1 + k))
                        for j in range(NPAIR):
                            last = mm(big[:, :], Ysc[:, j, tile_t(4 * half + k)], ST[:, j, :],
                                      start=j == 0, stop=j == NPAIR - 1)
                        used(last)
            norm_sums(2 * DEPTH)
            pe.wait_ge(sig["h_scaled"], (2 * DEPTH + 1) * KD)
            for t in range(NT):
                for half in range(2):
                    n = 2 * t + half
                    if n >= 2:
                        pe.wait_ge(sig["y_copied"], n - 1)
                    for k in range(4):
                        last = tr(W[2 + half][:, tile_t(k)], hT[:, 4 * half + k, tile_t(t)], ident)
                    last.then_inc(sig["y_turned"], 1)

        @block.scalar
        def _(act):
            a_ = nc.scalar.activation
            ch = Chain(act, sig["act_chain"])
            eps = C("eps")

            act.dma_start(xtok[:, 0:NTS, :], A["x_sample"][0].rearrange("(t p) d -> p t d", p=P))\
                .then_inc(sig["x_loaded"], 16)
            act.dma_start(xtok[:, NTS, :], A["x_prompt"][0]).then_inc(sig["x_loaded"], 16)

            def unit(n):
                act.wait_ge(sig["unit_computed"], n + 1)
                return ps[n % 2]

            def emptied(ins):
                ins.then_inc(sig["unit_emptied"], 1)

            def copy_context(n, dst, f=ACT.Copy):
                emptied(a_(dst, h4(unit(n)), f))

            def copy_unit(n, dst, f=ACT.Copy):
                emptied(a_(dst, unit(n)[:, :], f))

            def ada(l, a):
                n = unit_no(l, "ada", a)
                big = unit(n)
                emptied(a_(mod[:, 4 * a:4 * a + 4, :], big[:, 0:8].rearrange("p (m g) -> p m g", g=2), ACT.Copy))

            def norm(n):
                if n:
                    act.wait_ge(sig["x_added"], 10 * n)
                else:
                    act.wait_ge(sig["unit_emptied"], FIRST_UNITS)
                for k in range(KD):
                    if k >= 2:
                        act.wait_ge(sig["square_summed"], n * KD + k - 1)
                    a_(sqb[:, k % 2, :], xT[:, k, :], ACT.Square).then_inc(sig["squared"], 1)
                act.wait_ge(sig["square_summed"], (n + 1) * KD)
                act.wait_ge(sig["consts_loaded"], 16)
                a_(rt[:, 0, 0:TS], W[0][:, :], ACT.Sqrt, bias=eps, scale=1.0 / D)
                a_(rt[:, 0, TS:T], W[1][:, 0:TP], ACT.Sqrt, bias=eps, scale=1.0 / D).then_inc(sig["rooted"], 1)

            def shift(n, base):
                for k in range(KD):
                    act.wait_ge(sig["h_scaled"], n * KD + k + 1)
                    for g, cols in GRP:
                        last = a_(hT[:, k, cols], hT[:, k, cols], ACT.Identity, bias=mod[:, base + k, g:g + 1])
                    last.then_inc(sig["h_ready"], 1)

            act.wait_ge(sig["cond_loaded"], 48)
            a_(crow[0:16, :], crow[0:16, :], ACT.Silu).then_inc(sig["cond_silu"], 1)
            for k in range(KD):
                copy_unit(k, xT[:, k, 0:TS])
            for half in range(2):
                copy_context(KD + half, xT[:, 4 * half:4 * half + 4, TS:T])

            for l in range(DEPTH):
                for a in range(4):
                    ada(l, a)
                norm(2 * l)
                shift(2 * l, 0)
                def conv_silu(m):
                    act.wait_ge(sig["conv_done"], 12 * l + m + 1)
                    i, h = m // H, m % H
                    a_(cT[i][:, h, 0:TS], cvt[:, m % 2, 0:TS], ACT.Silu)
                    a_(cT[i][:, h, TS:T], cvt[:, m % 2, TS + 4:T + 4], ACT.Silu).then_inc(sig["conv_silu"], 1)

                for i, s in enumerate(("qb", "kb", "vb")):
                    if i == 2:
                        act.wait_ge(sig["conv_done"], 12 * l + H)
                    dst = pre[:, (i % 2) * H:(i % 2 + 1) * H, :]
                    copy_context(unit_no(l, s), dst[:, :, TS + 6:T + 6])
                    for h in range(H):
                        copy_unit(unit_no(l, s, 0, 1 + h), dst[:, h, 2:2 + TS])
                        if i or h:
                            conv_silu(H * i + h - 1)
                    ada(l, 4 + i)
                copy_context(unit_no(l, "zb"), obT[:, :, TS:T], ACT.Silu)
                conv_silu(11)
                for h in range(H):
                    copy_unit(unit_no(l, "zb", 0, 1 + h), obT[:, h, 0:TS], ACT.Silu)
                ada(l, 7)
                act.wait_ge(sig["small_loaded"], 80 * (l + 1))
                a_(nega, al, ACT.Exp).then_inc(sig["decay_rate"], 1)
                act.wait_ge(sig["dt_abs"], l + 1)
                ch.link(a_(gt2_, gt2_, ACT.Exp, scale=-1.0))
                a_(gt2_, gt2_, ACT.Ln, bias=1.0).then_inc(sig["dt_log"], 1)
                a_(beta, beta, ACT.Sigmoid)\
                    .then_inc(sig["beta_ready"], 1)
                for j in range(2 * H):
                    n = 2 * H * l + j
                    if j == 0:
                        act.wait_ge(sig["conv_silu"], 12 * (l + 1))
                    if j >= 2:
                        act.wait_ge(sig["qk_summed"], n - 1)
                    a_(sqb[:, j % 2, :], cT[j // H][:, j % H, :], ACT.Square).then_inc(sig["qk_squared"], 1)
                    if j:
                        m = n - 1
                        act.wait_ge(sig["qk_summed"], m + 1)
                        if j - 1 >= 2:
                            act.wait_ge(sig["qk_scaled"], m - 1)
                        a_(rt[:, (j - 1) % 2, 0:TS], W[2 * ((j - 1) % 2)][:, :], ACT.Sqrt, bias=eps)
                        a_(rt[:, (j - 1) % 2, TS:T], W[2 * ((j - 1) % 2) + 1][:, 0:TP], ACT.Sqrt, bias=eps)\
                            .then_inc(sig["qk_rooted"], 1)
                m = 2 * H * (l + 1) - 1
                act.wait_ge(sig["qk_summed"], m + 1)
                act.wait_ge(sig["qk_scaled"], m - 1)
                a_(rt[:, 1, 0:TS], W[2][:, :], ACT.Sqrt, bias=eps)
                a_(rt[:, 1, TS:T], W[3][:, 0:TP], ACT.Sqrt, bias=eps).then_inc(sig["qk_rooted"], 1)
                for t in range(NT):
                    act.wait_ge(sig["kv_turned"], NT * l + t + 1)
                    a_(ktok[:, t, :], W[0][:, :], ACT.Copy).then_inc(sig["ktok_ready"], 1)
                for i, (d, t) in enumerate(GROUPS):
                    n = NG * l + i
                    act.wait_ge(sig["gdiff_ready"], n + 1)
                    a_(gE, gE, ACT.Exp, scale=-1.0).then_inc(sig["decay_ready"], 1)
                    a_(eg, gcum, ACT.Exp)
                    a_(egl, glast, ACT.Exp)
                    a_(kds, gdif, ACT.Exp).then_inc(sig["decays_ready"], 1)
                    act.wait_ge(sig["la_turned"], n + 1)
                    a_(gLT, h4(W[0]), ACT.Copy).then_inc(sig["lt_ready"], 1)
                    a_(gAT, h4(W[3]), ACT.Copy).then_inc(sig["at_ready"], 1)
                    act.wait_ge(sig["d2_computed"], n + 1)
                    a_(gD2, h4(W[1]), ACT.Copy).then_inc(sig["d2_ready"], 1)
                    act.wait_ge(sig["d4_computed"], n + 1)
                    a_(gD4, h4(W[1]), ACT.Copy).then_inc(sig["d4_ready"], 1)
                    act.wait_ge(sig["d8_computed"], n + 1)
                    a_(gD2T, h4(W[1]), ACT.Copy).then_inc(sig["d8t_ready"], 1)
                    act.wait_ge(sig["x3_turned"], n + 1)
                    a_(gD, h4(W[1]), ACT.Copy).then_inc(sig["s0_ready"], 1)
                    for s in range(3):
                        act.wait_ge(sig["ct_computed"], 3 * n + s + 1)
                        a_(gD2, h4(W[2]), ACT.Copy).then_inc(sig["y_ready"], 1)
                    act.wait_ge(sig["w_computed"], n + 1)
                    a_(gDT, h4(W[1]), ACT.Copy, scale=-1.0).then_inc(sig["w_ready"], 1)
                    act.wait_ge(sig["vnew_computed"], n + 1)
                    a_(gD4, h4(W[0]), ACT.Copy).then_inc(sig["vnew_ready"], 1)
                for d in range(2):
                    act.wait_ge(sig["state_updated"], NG * (l + 1))
                    act.dma_start(O["new_state_delta"][0, l, d].rearrange("h k v -> k h v"), state[2 + d])\
                        .then_inc(sig["state_stored"], 16)
                act.wait_ge(sig["o_summed"], l + 1)
                a_(orms, orms, ACT.Sqrt, bias=eps, scale=1.0 / P).then_inc(sig["o_rooted"], 1)

                act.wait_ge(sig["delta_turned"], H * (l + 1))
                act.wait_ge(sig["state_stored"], 32 * (l + 1))
                act.wait_ge(sig["lam_dots"], l + 1)
                a_(lam4[:, 2:4], lam4[:, 0:2], ACT.Exp).then_inc(sig["lam_exp"], 1)
                for br in range(2):
                    nb = 2 * l + br
                    names = ("qa", "ka", "va") if br == 0 else ("qc", "kc", "vc")
                    if br == 1:
                        act.wait_ge(sig["attn_out"], 2 * H * nb)
                        act.wait_ge(sig["new_v_stored"], 16 * nb)
                    copy_context(unit_no(l, names[0]), aQ[:, :, TS:T])
                    for h in range(H):
                        copy_unit(unit_no(l, names[0], 0, 1 + h), aQ[:, h, 0:TS])
                    ada(l, 8 if br == 0 else 11)
                    copy_context(unit_no(l, names[1]), aK[:, :, TS:T])
                    for h in range(H):
                        copy_unit(unit_no(l, names[1], 0, 1 + h), aK[:, h, 0:TS])
                    if br == 0:
                        ada(l, 9)
                    for t in range(NT):
                        copy_unit(unit_no(l, names[2], 0, t), aV[:, t, :])
                    if br == 0:
                        ada(l, 10)
                    act.wait_ge(sig["unit_emptied"], unit_no(l, names[2], 0, NT))
                    act.dma_start(O["new_diff_v" if br == 0 else "new_na_v"][0, l].rearrange("t h d -> t (h d)"),
                                  aV[:, NTS, :]).then_inc(sig["new_v_stored"], 16)
                    act.wait_ge(sig["keys_turned"], nb + 1)
                    a_(ckT, h4(W[3]), ACT.Copy).then_inc(sig["keys_ready"], 1)
                    if nb:
                        act.wait_ge(sig["new_k_stored"], 16 * nb)
                    a_(ktp, W[4][:, :], ACT.Copy).then_inc(sig["new_k_copied"], 1)
                    act.wait_ge(sig["new_k_copied"], nb + 1)
                    act.dma_start(O["new_diff_k" if br == 0 else "new_na_k"][0, l].rearrange("t h d -> t (h d)"),
                                  ktp).then_inc(sig["new_k_stored"], 16)
                    for i, (h, qt) in enumerate(AUNITS):
                        n = NA * nb + i
                        scale = 0.125 if br == 0 else 1.0
                        act.wait_ge(sig["maxima_ready"], n + 1)
                        if br == 0:
                            for c in range(2):
                                if qt < NTS:
                                    a_(prob[:, c, 0:TS], W[c][:, :], ACT.Exp, bias=nm[:, c:c + 1], scale=scale,
                                       accum_out=rs[:, c:c + 1])
                                last = a_(prob[:, c, TS:T], W[2 + 3 * c][:, 0:P], ACT.Exp, bias=nm[:, c:c + 1],
                                          scale=scale, accum_out=rs[:, 2 + c:3 + c])
                            last.then_inc(sig["exps_ready"], 1)
                        else:
                            s0 = 0 if qt < NTS else TS
                            a_(prob[:, 0, s0:T], prob[:, 0, s0:T], ACT.Exp, bias=nm[:, 0:1],
                               accum_out=rs[:, 0:1]).then_inc(sig["exps_ready"], 1)
                        act.wait_ge(sig["probs_turned"], n + 1)
                        if qt < NTS:
                            a_(aT[:, 0:NTS, tile_t(qt)], h4(W[3]), ACT.Copy)
                            a_(aT[:, NTS, tile_t(qt)], W[4][:, 0:P], ACT.Copy).then_inc(sig["probs_copied"], 1)
                        else:
                            a_(aT[:, NTS, 0:P], W[4][:, 0:P], ACT.Copy).then_inc(sig["probs_copied"], 1)
                        if qt >= NTS - 1:
                            m = 2 * (H * nb + h) + (qt - NTS + 1)
                            cols = slice(0, TS) if qt < NTS else slice(TS, T)
                            wid = cols.stop - cols.start
                            act.wait_ge(sig["pv_computed"], m + 1)
                            if br == 0:
                                a_(sq1[:, cols], W[0][:, 0:wid], ACT.Square).then_inc(sig["sub_squared"], 1)
                                act.wait_ge(sig["sub_summed"], 2 * (H * l + h) + (qt - NTS + 1) + 1)
                                a_(rt1[:, cols], W[1][:, 0:wid], ACT.Sqrt, bias=eps, scale=1.0 / P)\
                                    .then_inc(sig["sub_rooted"], 1)

                act.wait_ge(sig["attn_out"], 2 * H * (2 * l + 2))
                act.wait_ge(sig["new_v_stored"], 32 * (l + 1))
                act.wait_ge(sig["new_k_stored"], 32 * (l + 1))
                for b, s in enumerate("abc"):
                    for half in range(2):
                        g = 2 * b + half
                        if g:
                            act.wait_ge(sig["merged_ready"], 5 * (6 * l + g))
                        copy_context(unit_no(l, "g" + s, half), gsig[:, :, TS:T], ACT.Sigmoid)
                        for m in range(4):
                            copy_unit(unit_no(l, "g" + s, half, 1 + m), gsig[:, m, 0:TS], ACT.Sigmoid)
                        copy_context(unit_no(l, "br" + s, half), brsp)
                        for m in range(4):
                            if m >= 2:
                                act.wait_ge(sig["merged_ready"], 5 * (6 * l + g) + m)
                            copy_unit(unit_no(l, "br" + s, half, 1 + m), brs[:, m % 2, :])
                act.wait_ge(sig["mod2_ready"], l + 1)

                def gate_units(name, i, j, half, v, gbase):
                    n = unit_no(l, name, i, j)
                    if half:
                        act.wait_ge(sig["x_added"], v)
                    bank = unit(n)
                    for k in range(4):
                        last = a_(xtmpp[:, k, :], bank[:, tile_t(k)], ACT.Copy,
                                  scale=mod[:, gbase + 4 * half + k, 1:2])
                    emptied(last)
                    for k in range(4):
                        if k >= 2:
                            act.wait_ge(sig["x_added"], v + k)
                        emptied(a_(xtmp[:, k % 2, :], unit(n + 1 + k)[:, :], ACT.Copy,
                                   scale=mod[:, gbase + 4 * half + k, 0:1]))

                for half in range(2):
                    gate_units("wo", half, 0, half, 20 * l + 5 * half, 16)
                norm(2 * l + 1)
                shift(2 * l + 1, 24)
                for half in range(2 * NT):
                    n = 2 * NT * l + half
                    act.wait_ge(sig["h2_turned"], n + 1)
                    a_(h2tok[:, half // 2, (half % 2) * 512:(half % 2) * 512 + 512], W[1 + half % 2][:, :], ACT.Copy)\
                        .then_inc(sig["h2_copied"], 1)
                    if half == 1:
                        act.wait_ge(sig["logits_shifted"], l + 1)
                        a_(aff, affs, ACT.Exp).then_inc(sig["logits_exp"], 1)
                for i in range(3 * KD):
                    n = 3 * KD * l + i
                    k, part = i // 3, i % 3
                    if i == 0:
                        act.wait_ge(sig["spread_ready"], (NPAIR + 2) * (l + 1))
                    act.wait_ge(sig["gather_computed"], n + 1)
                    if part < 2:
                        last = a_(XE[:, 8 * part:8 * part + 8, k, 0:SLS],
                                  W[i % 4][:, :].rearrange("p (e s) -> p e s", e=8), ACT.Copy)
                    else:
                        last = a_(XE[:, :, k, SLS:SL], W[i % 4][:, 0:NE * SLP].rearrange("p (e s) -> p e s", e=NE),
                                  ACT.Copy)
                    last.then_inc(sig["gathered"], 1)
                ub = unit_no(l, "pair")
                hb = NE * 2 * l
                act.wait_ge(sig["slotgate_ready"], l + 1)
                with act.Fori(0, NPAIR) as j:
                    def loop_unit(q):
                        act.wait_ge(sig["unit_computed"], j * PAIR_UNITS + (ub + q + 1))
                        return ps[(ub + q) % 2]

                    for x in range(2):
                        for part in range(6):
                            q = 6 * x + part
                            big = loop_unit(q)
                            half = part // 2 % 2
                            if part < 4:
                                if part % 2 == 0:
                                    act.wait_ge(sig["hidden_ready"], j * 4 + (hb + 2 * x + half + 1))
                                f, dst = (ACT.Silu, hgate) if part % 2 == 0 else (ACT.Copy, hup)
                                emptied(a_(dst[:, half, :], big[:, 0:4 * SL], f))
                            else:
                                half = part - 4
                                src = big[:, 0:4 * SL].rearrange("p (m s) -> p m s", m=4)
                                a_(yTs[:, 4 * half:4 * half + 4, x * SLS:(x + 1) * SLS], src[:, :, 0:SLS], ACT.Copy)
                                emptied(a_(yTp[:, 4 * half:4 * half + 4, bass.ds((2 * j + x) * SLP, SLP)],
                                           src[:, :, SLS:SL], ACT.Copy))
                    for half in range(2):
                        big = loop_unit(12 + half)
                        emptied(a_(Ysc[:, bass.ds(j, 1), 512 * half:512 * half + 512], big[:, :].unsqueeze(1), ACT.Copy))
                for i in range(4):
                    bank = unit(unit_no(l, "yp", 0, i))
                    emptied(a_(YP[:, i // 2, 512 * (i % 2):512 * (i % 2) + 512], bank[:, :], ACT.Copy,
                               scale=gslp[:, i // 2:i // 2 + 1]))
                for half in range(2):
                    gate_units("scatter", 0, 5 * half, half, 20 * l + 10 + 5 * half, 40)
            norm(2 * DEPTH)
            for n in range(2 * NT):
                act.wait_ge(sig["y_turned"], n + 1)
                t, half = n // 2, n % 2
                if t >= 2 and half == 0:
                    act.wait_ge(sig[f"y{t % 2}_stored"], 16 * (t // 2))
                a_(ytok[:, t % 2, 512 * half:512 * half + 512], W[2 + half][:, :], ACT.Copy).then_inc(sig["y_copied"], 1)
                if half:
                    act.wait_ge(sig["y_copied"], n + 1)
                    dst = O["y_sample"][0, tile_t(t), :] if t < NTS else O["y_prompt"][0]
                    act.dma_start(dst, ytok[:, t % 2, :]).then_inc(sig[f"y{t % 2}_stored"], 16)
            act.wait_ge(sig["y0_stored"], 16 * ((NT + 1) // 2))
            act.wait_ge(sig["y1_stored"], 16 * (NT // 2))
            act.wait_ge(sig["new_k_stored"], 32 * DEPTH)
            act.wait_ge(sig["new_v_stored"], 32 * DEPTH)
            act.wait_ge(sig["state_stored"], 32 * DEPTH)
            act.wait_ge(sig["rpb_padded"], 16 * DEPTH)

        @block.vector
        def _(dve):
            v_ = nc.vector
            ch = Chain(dve, sig["vec_chain"])
            TT, TSC, STT = v_.tensor_tensor, v_.tensor_scalar, v_.scalar_tensor_tensor

            def cols4(x, w=P):
                return x.unsqueeze(2).to_broadcast([P, H, w])

            def heads(m):
                return m.unsqueeze(1).to_broadcast([P, H, P])

            def norm_scale(n, col):
                dve.wait_ge(sig["rooted"], n + 1)
                ch.link(v_.reciprocal(rt[:, 0, :], rt[:, 0, :]))
                for k in range(KD):
                    for g, cols in GRP:
                        last = STT(hT[:, k, cols], xT[:, k, cols], col(k, g), rt[:, 0, cols], ALU.mult, ALU.mult)
                    last.then_inc(sig["h_scaled"], 1)

            v_.memset(ones[:, :], 1.0).then_inc(sig["ones_ready"], 1)
            for i in range(2):
                v_.memset(mx, 0.0).then_inc(sig["hidden_ready"], 1)
                dve.wait_ge(sig["hidden_ready"], i + 1)
            dve.wait_ge(sig["cond_turned"], 1)
            v_.tensor_copy(ccol[:, :], W[0][:, 0:24]).then_inc(sig["cond_ready"], 1)
            dve.wait_ge(sig["consts_loaded"], 16)
            for l in range(DEPTH):
                lam0 = 0.8 - 0.6 * math.exp(-0.3 * l)
                dve.wait_ge(sig["vectors_turned"], l + 1)
                ch.link(v_.tensor_copy(vcol[:, :], W[2][:, 0:V_ROWS]))
                dve.wait_ge(sig["unit_emptied"], unit_no(l, "ada", 3, 1))
                ch.link(TT(mod[:, 0:16, :], mod[:, 0:16, :],
                           vcol[:, 0:16].unsqueeze(2).to_broadcast([P, 16, 2]), ALU.add))
                ch.link(STT(amod[:, 0], mod[:, 8:16, :], 1.0, vcol[:, V_G1:V_G1 + 8].unsqueeze(2).to_broadcast([P, KD, 2]),
                            ALU.add, ALU.mult))
                norm_scale(2 * l, lambda k, g: amod[:, 0, k, g:g + 1])
                for a, b in ((0, 2), (TS + 2, TS + 6), (T + 6, T + 8)):
                    ch.mark(v_.memset(pre[:, :, a:b], 0.0))
                for s in range(2):
                    ins = v_.memset(state[2 + s], 0.0)
                    if s:
                        ins.then_inc(sig["state_zeroed"], 1)
                ch.wait()
                for i, s in enumerate(("qb", "kb", "vb")):
                    for h in range(H):
                        m = H * i + h
                        dve.wait_ge(sig["unit_emptied"], unit_no(l, s, 0, 1 + h) + 1)
                        if m >= 2:
                            dve.wait_ge(sig["conv_silu"], 12 * l + m - 1)
                        src, dst = pre[:, (i % 2) * H + h, :], cvt[:, m % 2, :]
                        taps = [vcol[:, V_CONV + 12 * j + m:V_CONV + 12 * j + m + 1] for j in range(CONV)]
                        ch.link(TSC(dst, src[:, 0:T + 4], taps[0], None, ALU.mult))
                        for j in range(1, CONV):
                            last = STT(dst, src[:, j:j + T + 4], taps[j], dst, ALU.mult, ALU.add)
                            if j < CONV - 1:
                                ch.link(last)
                        last.then_inc(sig["conv_done"], 1)
                dve.wait_ge(sig["ab_computed"], l + 1)
                dve.wait_ge(sig["small_loaded"], 80 * (l + 1))
                ab = W[4][:, 0:80].rearrange("p (t c) -> p t c", t=NT)
                ch.mark(v_.tensor_copy(beta, ab[:, :, 8:16]))
                ch.link(TT(gt1_, ab[:, :, 0:8], dtb.unsqueeze(1).to_broadcast([P, NT, 8]), ALU.add))
                STT(gt2_, gt1_, -1.0, gt1_, ALU.mult, ALU.max).then_inc(sig["dt_abs"], 1)
                dve.wait_ge(sig["dt_log"], l + 1)
                dve.wait_ge(sig["decay_rate"], l + 1)
                ch.link(STT(gt1_, gt1_, 0.0, gt2_, ALU.max, ALU.add))
                STT(gg, gt1_, -1.0, nega.unsqueeze(1).to_broadcast([P, NT, 8]), ALU.mult, ALU.mult)\
                    .then_inc(sig["g_ready"], 1)
                for j in range(2 * H):
                    n = 2 * H * l + j
                    dve.wait_ge(sig["qk_rooted"], n + 1)
                    ch.link(v_.reciprocal(rt[:, j % 2, :], rt[:, j % 2, :]))
                    x = cT[j // H][:, j % H, :]
                    STT(x, x, P ** -0.5 if j < H else 1.0, rt[:, j % 2, :], ALU.mult, ALU.mult)\
                        .then_inc(sig["qk_scaled"], 1)
                for t in range(NT):
                    dve.wait_ge(sig["kv_turned"], NT * l + t + 1)
                    v_.tensor_copy(vtok[:, t, :], W[1][:, :]).then_inc(sig["vtok_ready"], 1)
                dve.wait_ge(sig["ktok_ready"], NT * (l + 1))
                dve.wait_ge(sig["vtok_ready"], NT * (l + 1))
                dve.wait_ge(sig["beta_ready"], l + 1)
                for i, (d, t) in enumerate(GROUPS):
                    n = NG * l + i
                    st = state[d + (2 if t == NTS else 0)]
                    end = P - 1 if d == 0 else 0
                    bt = beta[:, t, 4 * d:4 * d + 4]
                    dve.wait_ge(sig["gsum_computed"], n + 1)
                    ch.mark(v_.tensor_copy(gcum, W[3][:, 0:4]))
                    ch.link(v_.tensor_copy(glast, h4(W[0])[:, :, end]))
                    ch.mark(TT(gdif, glast, gcum, ALU.subtract))
                    for h in range(H):
                        last = TSC(gE[:, h, :], W[0][:, tile_t(h)], gcum[:, h:h + 1], 0.0, ALU.subtract, ALU.max)
                    last.then_inc(sig["gdiff_ready"], 1)
                    vt3 = vtok[:, t, :].rearrange("p (h c) -> p h c", h=H)
                    kt3 = ktok[:, t, :].rearrange("p (h c) -> p h c", h=H)
                    ch.mark(TT(gVB, vt3, cols4(bt), ALU.mult))
                    dve.wait_ge(sig["decay_ready"], n + 1)
                    dve.wait_ge(sig["kk_computed"], n + 1)
                    ch.mark(TT(gL, gE, heads(C("strict")[:, d * P:(d + 1) * P]), ALU.mult))
                    ch.link(TT(gA, gE, heads(C("tri")[:, d * P:(d + 1) * P]), ALU.mult))
                    ch.link(TT(gL, gL, h4(W[1]), ALU.mult))
                    ch.mark(TT(gL, gL, cols4(bt), ALU.mult))
                    TT(gA, gA, h4(W[2]), ALU.mult).then_inc(sig["la_ready"], 1)
                    dve.wait_ge(sig["decays_ready"], n + 1)
                    ch.wait()
                    ch.mark(TT(gD, gL, heads(C("blk16")), ALU.mult))
                    ch.link(TT(bexp, bt, eg, ALU.mult))
                    ch.link(TT(gX, heads(ident), gD, ALU.subtract))
                    dve.wait_ge(sig["lt_ready"], n + 1)
                    TT(gDT, gLT, heads(C("blk16")), ALU.mult).then_inc(sig["d_ready"], 1)
                    ch.mark(TT(gKB, kt3, cols4(bexp), ALU.mult))
                    dve.wait_ge(sig["d2_computed"], n + 1)
                    v_.tensor_copy(gD2T, h4(W[2])).then_inc(sig["d2t_ready"], 1)
                    ch.mark(TT(gKD, kt3, cols4(kds), ALU.mult))
                    dve.wait_ge(sig["d4_computed"], n + 1)
                    ch.mark(v_.tensor_copy(gD4T, h4(W[2])))
                    TT(gX, gX, h4(W[4]), ALU.add).then_inc(sig["x1_ready"], 1)
                    ch.mark(TT(c32, gLT, heads(C("m32")), ALU.mult))
                    dve.wait_ge(sig["x1_ready"], n + 1)
                    dve.wait_ge(sig["d8_computed"], n + 1)
                    TT(gX, gX, h4(W[2]), ALU.add).then_inc(sig["x2_ready"], 1)
                    ch.mark(TT(c64, gLT, heads(C("m64")), ALU.mult))
                    dve.wait_ge(sig["x2_ready"], n + 1)
                    dve.wait_ge(sig["x3_computed"], n + 1)
                    TT(gX, gX, h4(W[4]), ALU.add).then_inc(sig["x3_ready"], 1)
                    ch.link(TT(c128, gLT, heads(C("m128")), ALU.mult))
                    dve.wait_ge(sig["x3_ready"], n + 1)
                    dve.wait_ge(sig["s0_ready"], n + 1)
                    v_.tensor_copy(mx[:, 0:1], ident[:, 0:1]).then_inc(sig["s_ready"], 1)
                    for s in range(3):
                        dve.wait_ge(sig["tct_computed"], 3 * n + s + 1)
                        if s < 2:
                            ch.mark(TT(gX, gX, h4(W[1]), ALU.subtract))
                            TT(gD, gD, h4(W[4]), ALU.subtract).then_inc(sig["s_ready"], 1)
                            ch.wait()
                            dve.wait_ge(sig["s_ready"], 3 * n + s + 2)
                        else:
                            TT(gD, gD, h4(W[4]), ALU.subtract).then_inc(sig["inverse_ready"], 1)
                    dve.wait_ge(sig["qs_computed"], n + 1)
                    ch.link(TT(gL, h4(W[2]), cols4(eg), ALU.mult))
                    dve.wait_ge(sig["av_computed"], n + 1)
                    ch.link(TT(gL, gL, h4(W[3]), ALU.add))
                    ot = otok[:, t, :].rearrange("p (h c) -> p h c", h=H)
                    if ADDS[i]:
                        ch.mark(TT(ot, ot, gL, ALU.add))
                    else:
                        ch.mark(v_.tensor_copy(ot, gL))
                    for h in range(H):
                        last = STT(st[:, h, :], st[:, h, :], egl[:, h:h + 1], W[4][:, tile_t(h)], ALU.mult, ALU.add)
                    last.then_inc(sig["state_updated"], 1)
                    ch.wait()
                    dve.wait_ge(sig["state_updated"], n + 1)
                for t in range(NT):
                    ot = otok[:, t, :].rearrange("p (h c) -> p h c", h=H)
                    ch.link(TT(gL, ot, ot, ALU.mult))
                    last = v_.tensor_reduce(orms[:, 4 * t:4 * t + 4], gL, AX, ALU.add)
                    if t < NT - 1:
                        ch.link(last)
                last.then_inc(sig["o_summed"], 1)
                dve.wait_ge(sig["o_rooted"], l + 1)
                ch.link(v_.reciprocal(orms, orms))
                for t in range(NT):
                    ot = otok[:, t, :].rearrange("p (h c) -> p h c", h=H)
                    last = TT(ot, ot, cols4(orms[:, 4 * t:4 * t + 4]), ALU.mult)
                last.then_inc(sig["otok_ready"], 1)
                for h in range(H):
                    dve.wait_ge(sig["o_turned"], H * l + h + 1)
                    gcol = vcol[:, V_GO:V_GO + 1]
                    STT(obT[:, h, 0:TS], W[0][:, :], gcol, obT[:, h, 0:TS], ALU.mult, ALU.mult)
                    STT(obT[:, h, TS:T], W[1][:, 0:TP], gcol, obT[:, h, TS:T], ALU.mult, ALU.mult)\
                        .then_inc(sig["delta_turned"], 1)
                ch.link(TT(lq[:, 0:64], lq[:, 0:64], lq[:, 64:128], ALU.mult))
                ch.link(TT(lq[:, 128:192], lq[:, 128:192], lq[:, 192:256], ALU.mult))
                v_.tensor_reduce(lam4[:, 0:2], lq.rearrange("p (a b c) -> p a b c", a=2, b=2)[:, :, 0, :], AX, ALU.add)\
                    .then_inc(sig["lam_dots"], 1)

                for br in range(2):
                    nb = 2 * l + br
                    if br == 0:
                        for j in range(2 * H):
                            x = (aQ, aK)[j // H][:, j % H, 0:TS]
                            dve.wait_ge(sig["unit_emptied"], unit_no(l, "qa" if j < H else "ka", 0, 1 + j % H) + 1)
                            ch.mark(v_.stream_shuffle(rot, x, [(i + 16) % 32 for i in range(32)]))
                            ch.wait()
                            ch.mark(TT(rot, rot, C("sin"), ALU.mult))
                            ch.link(TT(x, x, C("cos"), ALU.mult))
                            TT(x, x, rot, ALU.add).then_inc(sig["rotated"], 1)
                            dve.wait_ge(sig["rotated"], 2 * H * l + j + 1)
                    else:
                        dve.wait_ge(sig["unit_emptied"], unit_no(l, "ada", 11, 1))
                        ch.link(TT(mod[:, 16:48, :], mod[:, 16:48, :],
                                   vcol[:, 16:48].unsqueeze(2).to_broadcast([P, 32, 2]), ALU.add))
                        STT(amod[:, 1], mod[:, 32:40, :], 1.0, vcol[:, V_G2:V_G2 + 8].unsqueeze(2).to_broadcast([P, KD, 2]),
                            ALU.add, ALU.mult).then_inc(sig["mod2_ready"], 1)
                    if br == 0:
                        dve.wait_ge(sig["lam_exp"], l + 1)
                        ch.link(TT(lamc, lam4[:, 3:4], lam4[:, 2:3], ALU.subtract))
                        ch.link(TSC(lamc, lamc, -lam0, None, ALU.add))
                    for i, (h, qt) in enumerate(AUNITS):
                        n = NA * nb + i
                        s0 = 0 if qt < NTS else TS
                        dve.wait_ge(sig["scores_computed"], n + 1)
                        if br == 0:
                            for c in range(2):
                                ch.mark(v_.tensor_reduce(mx[:, 2 + c:3 + c], W[2 + 3 * c][:, 0:P], AX, ALU.max))
                            if qt < NTS:
                                ch.mark(v_.tensor_reduce(mx[:, 0:1], W[0][:, :], AX, ALU.max))
                                ch.link(v_.tensor_reduce(mx[:, 1:2], W[1][:, :], AX, ALU.max))
                                ch.link(TT(mx[:, 2:4], mx[:, 0:2], mx[:, 2:4], ALU.max))
                            ch.wait()
                            TSC(nm, mx[:, 2:4], -0.125, None, ALU.mult).then_inc(sig["maxima_ready"], 1)
                            dve.wait_ge(sig["exps_ready"], n + 1)
                            if qt < NTS:
                                ch.link(TT(rs[:, 2:4], rs[:, 0:2], rs[:, 2:4], ALU.add))
                            ch.link(v_.reciprocal(cf[:, 0:2], rs[:, 2:4]))
                            ch.link(TT(cf[:, 1:2], cf[:, 1:2], lamc, ALU.mult))
                            ch.link(TSC(comb[:, s0:T], prob[:, 1, s0:T], cf[:, 1:2], None, ALU.mult))
                            STT(comb[:, s0:T], prob[:, 0, s0:T], cf[:, 0:1], comb[:, s0:T], ALU.mult, ALU.add)\
                                .then_inc(sig["probs_ready"], 1)
                        else:
                            if qt < NTS:
                                k = l * H * NTS + h * NTS + qt
                                dve.wait_ge(sig["bias_ready"], k + 1)
                                ch.mark(STT(prob[:, 0, 0:TS], W[0][:, :], P ** -0.5, bmt[:, k % 2, :],
                                            ALU.mult, ALU.add))
                            ch.link(TSC(prob[:, 0, TS:T], W[2][:, 0:P], P ** -0.5, None, ALU.mult))
                            if qt < NTS:
                                v_.tensor_reduce(mx[:, 0:1], prob[:, 0, s0:T], AX, ALU.max).then_inc(sig["bias_used"], 1)
                                dve.wait_ge(sig["bias_used"], k + 1)
                            else:
                                ch.link(v_.tensor_reduce(mx[:, 0:1], prob[:, 0, s0:T], AX, ALU.max))
                            TSC(nm[:, 0:1], mx[:, 0:1], -1.0, None, ALU.mult).then_inc(sig["maxima_ready"], 1)
                            dve.wait_ge(sig["exps_ready"], n + 1)
                            ch.link(v_.reciprocal(cf[:, 0:1], rs[:, 0:1]))
                            TSC(comb[:, s0:T], prob[:, 0, s0:T], cf[:, 0:1], None, ALU.mult)\
                                .then_inc(sig["probs_ready"], 1)
                        if qt >= NTS - 1:
                            m = 2 * (H * nb + h) + (qt - NTS + 1)
                            cols = slice(0, TS) if qt < NTS else slice(TS, T)
                            wid = cols.stop - cols.start
                            dve.wait_ge(sig["pv_computed"], m + 1)
                            if br == 0:
                                dve.wait_ge(sig["sub_rooted"], 2 * (H * l + h) + (qt - NTS + 1) + 1)
                                ch.link(v_.reciprocal(rt1[:, cols], rt1[:, cols]))
                                ch.link(TSC(rt1[:, cols], rt1[:, cols], vcol[:, V_GS:V_GS + 1], 1.0 - lam0,
                                            ALU.mult, ALU.mult))
                                TT(oaT[:, h, cols], W[0][:, 0:wid], rt1[:, cols], ALU.mult)\
                                    .then_inc(sig["attn_out"], 1)
                            else:
                                v_.tensor_copy(ocT[:, h, cols], W[0][:, 0:wid]).then_inc(sig["attn_out"], 1)

                for b in range(3):
                    for half in range(2):
                        def merge(dst, gate, prod):
                            if b == 0:
                                TT(dst, gate, prod, ALU.mult).then_inc(sig["merged_ready"], 1)
                            else:
                                ch.link(TT(prod, gate, prod, ALU.mult))
                                TT(dst, dst, prod, ALU.add).then_inc(sig["merged_ready"], 1)

                        n = unit_no(l, "br" + "abc"[b], half)
                        dve.wait_ge(sig["unit_emptied"], n + 1)
                        merge(merged[:, 4 * half:4 * half + 4, TS:T], gsig[:, :, TS:T], brsp)
                        for m in range(4):
                            dve.wait_ge(sig["unit_emptied"], n + 2 + m)
                            merge(merged[:, 4 * half + m, 0:TS], gsig[:, m, 0:TS], brs[:, m % 2, :])

                def add_x(n, half):
                    dve.wait_ge(sig["unit_emptied"], n + 1)
                    x = xT[:, 4 * half:4 * half + 4, :]
                    TT(x[:, :, TS:T], x[:, :, TS:T], xtmpp, ALU.add).then_inc(sig["x_added"], 1)
                    for k in range(4):
                        dve.wait_ge(sig["unit_emptied"], n + 2 + k)
                        TT(x[:, k, 0:TS], x[:, k, 0:TS], xtmp[:, k % 2, :], ALU.add).then_inc(sig["x_added"], 1)

                for half in range(2):
                    add_x(unit_no(l, "wo", half), half)
                dve.wait_ge(sig["mod2_ready"], l + 1)
                dve.wait_ge(sig["x_added"], 20 * l + 10)
                norm_scale(2 * l + 1, lambda k, g: amod[:, 1, k, g:g + 1])
                dve.wait_ge(sig["logits_computed"], l + 1)
                lg = W[0][:, 0:NT * NE].rearrange("p (t e) -> p t e", t=NT)
                ch.link(v_.tensor_reduce(sof, lg, AX, ALU.max))
                TT(affs, lg, sof.unsqueeze(2).to_broadcast([P, NT, NE]), ALU.subtract).then_inc(sig["logits_shifted"], 1)
                dve.wait_ge(sig["logits_exp"], l + 1)
                ch.link(v_.tensor_reduce(sof, aff, AX, ALU.add))
                ch.link(v_.reciprocal(sof, sof))
                TT(aff, aff, sof.unsqueeze(2).to_broadcast([P, NT, NE]), ALU.mult).then_inc(sig["aff_ready"], 1)
                dve.wait_ge(sig["aff_turned"], l + 1)
                ch.mark(v_.tensor_copy(affT[0:NE, 0:TS], W[3][0:NE, :]))
                ch.link(v_.tensor_copy(affT[0:NE, TS:T], W[4][0:NE, 0:TP]))
                for cols, n in ((slice(0, TS), SLS), (slice(TS, T), SLP)):
                    for _ in range(n // 8):
                        ch.link(v_.max(top8[0:NE, :], affT[0:NE, cols]))
                        ch.link(v_.match_replace(affT[0:NE, cols], top8[0:NE, :], affT[0:NE, cols], -1.0))
                ch.mark(v_.memset(onesr[0:NE, :], 1.0))
                for dst, w in ((sel, SLS), (selp, SLP)):
                    ch.mark(v_.tensor_copy(dst[0:NE, :].rearrange("p (e s) -> p e s", e=NE),
                                           ident[0:NE, 0:NE].unsqueeze(2).to_broadcast([NE, NE, w])))
                ch.link(TSC(msk[0:NE, :], affT[0:NE, :], 0.0, None, ALU.is_lt))
                for cols in (slice(0, TS), slice(TS, T)):
                    ch.link(v_.tensor_tensor_scan(posm[0:NE, cols], onesr[0:NE, cols], msk[0:NE, cols], 0.0,
                                                  ALU.mult, ALU.add))
                ch.link(TT(posm[0:NE, :], posm[0:NE, :], msk[0:NE, :], ALU.mult))
                TSC(posm[0:NE, :], posm[0:NE, :], -1.0, None, ALU.add).then_inc(sig["slots_ready"], 1)
                dve.wait_ge(sig["slots_turned"], l + 1)
                ch.link(v_.tensor_copy(post, W[0][:, 0:NT * NE].rearrange("p (t e) -> p t e", t=NT)))
                for t in range(NT):
                    w = SLS if t < NTS else SLP
                    dst = (oneh[:, t, :] if t < NTS else onehp).rearrange("p (e s) -> p e s", e=NE)
                    last = TT(dst, C("iota")[:, 0:w].unsqueeze(1).to_broadcast([P, NE, w]),
                              post[:, t, :].unsqueeze(2).to_broadcast([P, NE, w]), ALU.is_equal)
                last.then_inc(sig["onehot_ready"], 1)
                for j in range(NPAIR + 2):
                    n = (NPAIR + 2) * l + j
                    dve.wait_ge(sig["spread_computed"], n + 1)
                    if j < NPAIR:
                        last = TSC(ST[:, j, :], W[1 + j % 2][:, :], C("pm64"), None, ALU.is_equal)
                    else:
                        last = TSC(STP[:, j - NPAIR, :], W[1 + j % 2][:, 0:TP], C("pm16"), None, ALU.is_equal)
                    last.then_inc(sig["spread_ready"], 1)
                dve.wait_ge(sig["slotgate_computed"], l + 1)
                gm = C("gmask").rearrange("p (j e) -> p j e", e=NE)
                gmp = C("gmaskp").rearrange("p (j e) -> p j e", e=NE)
                tmp = msk[:, 0:NPAIR * NE].rearrange("p (j e) -> p j e", e=NE)
                tmpp = msk[:, NPAIR * NE:(NPAIR + 2) * NE].rearrange("p (j e) -> p j e", e=NE)
                ch.mark(TT(tmp, W[3][:, 0:NPAIR * NE].rearrange("p (j e) -> p j e", e=NE), gm, ALU.mult))
                ch.link(TT(tmpp, W[4][:, 0:2 * NE].rearrange("p (j e) -> p j e", e=NE), gmp, ALU.mult))
                ch.mark(v_.tensor_reduce(gsl, tmp, AX, ALU.add))
                v_.tensor_reduce(gslp, tmpp, AX, ALU.add).then_inc(sig["slotgate_ready"], 1)
                ub, hb = unit_no(l, "pair"), NE * 2 * l
                with dve.Fori(0, NPAIR) as j:
                    for x in range(2):
                        for half in range(2):
                            dve.wait_ge(sig["unit_emptied"], j * PAIR_UNITS + (ub + 6 * x + 2 * half + 2))
                            TT(hid[:, x, 4 * half * SL:4 * (half + 1) * SL], hgate[:, half, :], hup[:, half, :],
                               ALU.mult).then_inc(sig["hidden_ready"], 1)
                dve.wait_ge(sig["unit_emptied"], unit_no(l, "yp", 0, 4))
                ch.wait()
                for j in range(NPAIR):
                    last = TSC(Ysc[:, j, :], Ysc[:, j, :], gsl[:, j:j + 1], None, ALU.mult)
                last.then_inc(sig["yp_gated"], 1)
                for half in range(2):
                    add_x(unit_no(l, "scatter", 0, 5 * half), half)
                dve.wait_ge(sig["x_added"], 20 * (l + 1))
            norm_scale(2 * DEPTH, lambda k, g: ccol[:, 16 + k:17 + k])


_OUTS = [("y_prompt", (1, TP, D)), ("y_sample", (1, TS, D)), ("new_diff_k", (1, DEPTH, TP, H, P)),
         ("new_diff_v", (1, DEPTH, TP, H, P)), ("new_na_k", (1, DEPTH, TP, H, P)),
         ("new_na_v", (1, DEPTH, TP, H, P)), ("new_state_delta", (1, DEPTH, 2, H, P, P))]


def kernel(**inputs):
    import concourse.bacc as bacc
    from concourse.bass_utils import run_bass_kernel_spmd

    nc = bacc.Bacc("TRN2", target_bir_lowering=False, num_devices=1)
    arrays, A, O = {}, {}, {}
    for name, a in list(inputs.items()) + [("consts", constants())]:
        a = np.ascontiguousarray(a)
        arrays[f"in_{name}"] = a
        A[name] = nc.dram_tensor(f"in_{name}", a.shape, F32, kind="ExternalInput").ap()
    for name, shape in _OUTS:
        O[name] = nc.dram_tensor(f"out_{name}", shape, F32, kind="ExternalOutput").ap()
    build(nc, A, O)
    r = run_bass_kernel_spmd(nc, [arrays], core_ids=[0])
    return tuple(r.results[0][f"out_{name}"] for name, _ in _OUTS)
```
